# Optimizing a Trainium2 kernel written in Bass

```python
import math
import jax, jax.numpy as jnp
from jax import lax
import numpy as np

D_MODEL = 2048
BATCH = 1
SEQ = 256
DEPTH = 1

D_CONV = 512
N_CONV_GROUPS = 4
D_ATT = 1024
N_HEADS = 8
HEAD_DIM = 128
D_CFM = 512
N_CFM_GROUPS = 4
D_MIX = D_CONV + D_ATT + D_CFM
D_IN = 3 * D_CONV + 3 * D_ATT + 2 * D_CFM
SHORT_CONV_W = 3
CFM_CONV_W = 31
MOBA_BLOCK = 256
MOBA_TOPK = 3
Q_CHUNK = 64
N_GROUPS = 4
EXPERTS_PER_GROUP = 8
N_EXPERTS = N_GROUPS * EXPERTS_PER_GROUP
TOPK_IN_GROUP = 2
D_EXPERT = 512
ROW_BLOCK = 128
EPS = 1e-6
NEG = -1e30

kernel_name = 'hymba_parallel_conv_moba_conformer_hmoe'

def rmsnorm(x, g):
    x32 = x.astype(jnp.float32)
    y = x32 * lax.rsqrt(jnp.mean(x32 * x32, axis=-1, keepdims=True) + EPS)
    return (y * g.astype(jnp.float32)).astype(x.dtype)

def causal_depthwise_conv(x, w):
    width, ch = w.shape
    return lax.conv_general_dilated(
        x, w[:, None, :].astype(x.dtype), window_strides=(1,),
        padding=[(width - 1, 0)], dimension_numbers=('NWC', 'WIO', 'NWC'),
        feature_group_count=ch)

def alibi_slopes(n):
    return jnp.exp2(-8.0 * jnp.arange(1, n + 1, dtype=jnp.float32) / n)

def short_conv_mixer(u, conv_w):
    bg, cg, xv = jnp.split(u, 3, axis=-1)
    return bg * causal_depthwise_conv(cg * xv, conv_w)

def conformer_conv_mixer(u, conv_w, conv_b, ln_g, ln_b):
    a, gate = jnp.split(u, 2, axis=-1)
    h = a * jax.nn.sigmoid(gate)
    h = causal_depthwise_conv(h, conv_w) + conv_b.astype(h.dtype)
    h32 = h.astype(jnp.float32)
    mu = jnp.mean(h32, axis=-1, keepdims=True)
    var = jnp.mean(jnp.square(h32 - mu), axis=-1, keepdims=True)
    hn = (h32 - mu) * lax.rsqrt(var + EPS) * ln_g.astype(jnp.float32) + ln_b.astype(jnp.float32)
    return jax.nn.silu(hn).astype(u.dtype)

def moba_attention(q, k, v):
    bn, s, _ = q.shape
    nb = -(-s // MOBA_BLOCK)
    s_pad = nb * MOBA_BLOCK
    k_top = min(MOBA_TOPK, nb)
    n_chunks = s // Q_CHUNK

    def heads(t):
        return t.reshape(bn, s, N_HEADS, HEAD_DIM).transpose(0, 2, 1, 3)

    pad = ((0, 0), (0, 0), (0, s_pad - s), (0, 0))
    qh = heads(q) * (HEAD_DIM ** -0.5)
    kh = jnp.pad(heads(k), pad)
    vh = jnp.pad(heads(v), pad)
    kb = kh.reshape(bn, N_HEADS, nb, MOBA_BLOCK, HEAD_DIM)
    vb = vh.reshape(bn, N_HEADS, nb, MOBA_BLOCK, HEAD_DIM)
    kmean = jnp.mean(kb.astype(jnp.float32), axis=3)

    qblk = jnp.arange(s) // MOBA_BLOCK
    gate = jnp.einsum('bhsd,bhnd->bhsn', qh.astype(jnp.float32), kmean)
    fully_past = jnp.arange(nb)[None, :] < qblk[:, None]
    gate = jnp.where(fully_past, gate, NEG)
    _, sel = lax.top_k(gate, k_top)
    slopes = alibi_slopes(N_HEADS)

    def chunk(bc):
        b = bc // n_chunks
        t0 = (bc % n_chunks) * Q_CHUNK
        blk = t0 // MOBA_BLOCK
        qc = lax.dynamic_slice_in_dim(lax.dynamic_index_in_dim(qh, b, 0, False), t0, Q_CHUNK, 1)
        selc = lax.dynamic_slice_in_dim(lax.dynamic_index_in_dim(sel, b, 0, False), t0, Q_CHUNK, 1)
        kb_b = lax.dynamic_index_in_dim(kb, b, 0, False)
        vb_b = lax.dynamic_index_in_dim(vb, b, 0, False)
        gather = jax.vmap(lambda xh, ih: xh[ih])
        ks = gather(kb_b, selc)
        vs = gather(vb_b, selc)
        tpos = t0 + jnp.arange(Q_CHUNK)
        kpos = selc[..., None] * MOBA_BLOCK + jnp.arange(MOBA_BLOCK)
        valid = jnp.arange(k_top) < blk
        s_sel = jnp.einsum('hqd,hqrsd->hqrs', qc, ks).astype(jnp.float32)
        s_sel = s_sel - slopes[:, None, None, None] * (tpos[None, :, None, None] - kpos).astype(jnp.float32)
        s_sel = jnp.where(valid[None, None, :, None], s_sel, NEG)
        ko = lax.dynamic_slice_in_dim(lax.dynamic_index_in_dim(kh, b, 0, False), blk * MOBA_BLOCK, MOBA_BLOCK, 1)
        vo = lax.dynamic_slice_in_dim(lax.dynamic_index_in_dim(vh, b, 0, False), blk * MOBA_BLOCK, MOBA_BLOCK, 1)
        kpos_own = blk * MOBA_BLOCK + jnp.arange(MOBA_BLOCK)
        s_own = jnp.einsum('hqd,hsd->hqs', qc, ko).astype(jnp.float32)
        s_own = s_own - slopes[:, None, None] * (tpos[:, None] - kpos_own[None, :]).astype(jnp.float32)
        s_own = jnp.where(kpos_own[None, :] <= tpos[:, None], s_own, NEG)
        logits = jnp.concatenate([s_sel.reshape(N_HEADS, Q_CHUNK, k_top * MOBA_BLOCK), s_own], axis=-1)
        p = jax.nn.softmax(logits, axis=-1)
        p_sel = p[..., :k_top * MOBA_BLOCK].reshape(N_HEADS, Q_CHUNK, k_top, MOBA_BLOCK).astype(vs.dtype)
        p_own = p[..., k_top * MOBA_BLOCK:].astype(vo.dtype)
        return jnp.einsum('hqrs,hqrsd->hqd', p_sel, vs) + jnp.einsum('hqs,hsd->hqd', p_own, vo)

    o = lax.map(chunk, jnp.arange(bn * n_chunks))
    o = o.reshape(bn, n_chunks, N_HEADS, Q_CHUNK, HEAD_DIM).transpose(0, 1, 3, 2, 4)
    return o.reshape(bn, s, D_ATT)

def hierarchical_moe(x, rg_w, rg_b, re_w, re_b, w_gate, w_up, w_down):
    bn, s, d = x.shape
    t = bn * s
    xt = x.reshape(t, d)
    pg = jax.nn.softmax((xt @ rg_w).astype(jnp.float32) + rg_b.astype(jnp.float32), axis=-1)
    grp = jnp.argmax(pg, axis=-1)
    p_grp = jnp.take_along_axis(pg, grp[:, None], axis=1)[:, 0]
    le = ((xt @ re_w).astype(jnp.float32) + re_b.astype(jnp.float32)).reshape(t, N_GROUPS, EXPERTS_PER_GROUP)
    le_g = jnp.take_along_axis(le, grp[:, None, None], axis=1)[:, 0]
    q_top, e_top = lax.top_k(jax.nn.softmax(le_g, axis=-1), TOPK_IN_GROUP)
    gates = p_grp[:, None] * q_top / jnp.sum(q_top, axis=-1, keepdims=True)
    expert = grp[:, None] * EXPERTS_PER_GROUP + e_top

    n_assign = t * TOPK_IN_GROUP
    e_flat = expert.reshape(-1)
    g_flat = gates.reshape(-1)
    tok_flat = jnp.repeat(jnp.arange(t, dtype=jnp.int32), TOPK_IN_GROUP)
    order = jnp.argsort(e_flat)
    e_s, tok_s, g_s = e_flat[order], tok_flat[order], g_flat[order]
    counts = jnp.bincount(e_flat, length=N_EXPERTS)
    padded = (counts + ROW_BLOCK - 1) // ROW_BLOCK * ROW_BLOCK
    start = jnp.cumsum(counts) - counts
    end_p = jnp.cumsum(padded)
    start_p = end_p - padded
    dest = start_p[e_s] + (jnp.arange(n_assign) - start[e_s])
    n_rows = n_assign + N_EXPERTS * ROW_BLOCK
    n_blocks = n_rows // ROW_BLOCK
    row_tok = jnp.zeros((n_rows,), jnp.int32).at[dest].set(tok_s)
    row_w = jnp.zeros((n_rows,), jnp.float32).at[dest].set(g_s)
    blk_expert = jnp.clip(jnp.searchsorted(end_p, jnp.arange(n_blocks) * ROW_BLOCK, side='right'), 0, N_EXPERTS - 1)

    def expert_block(args):
        tok, e = args
        xb = xt[tok]
        h = jax.nn.silu(xb @ w_gate[e]) * (xb @ w_up[e])
        return h @ w_down[e]

    y = lax.map(expert_block, (row_tok.reshape(n_blocks, ROW_BLOCK), blk_expert))
    y = y.reshape(n_rows, d) * row_w[:, None].astype(y.dtype)
    out = jax.ops.segment_sum(y, row_tok, num_segments=t)
    return out.reshape(bn, s, d).astype(x.dtype)

def setup_inputs(seed: int = 0) -> dict:
    key = jax.random.key(seed)
    ks = jax.random.split(key, 20)
    L, D = DEPTH, D_MODEL

    def nrm(k, shape, scale):
        return jax.random.normal(k, shape, jnp.float32) * scale

    return {
        'x': nrm(ks[0], (BATCH, SEQ, D), 1.0),
        'norm1_g': 1.0 + nrm(ks[1], (L, D), 0.01),
        'w_in': nrm(ks[2], (L, D, D_IN), D ** -0.5),
        'conv_a_w': nrm(ks[3], (L, SHORT_CONV_W, D_CONV), SHORT_CONV_W ** -0.5),
        'conv_c_w': nrm(ks[4], (L, CFM_CONV_W, D_CFM), CFM_CONV_W ** -0.5),
        'conv_c_b': nrm(ks[5], (L, D_CFM), 0.01),
        'ln_c_g': 1.0 + nrm(ks[6], (L, D_CFM), 0.01),
        'ln_c_b': nrm(ks[7], (L, D_CFM), 0.01),
        'w_out': nrm(ks[8], (L, D_MIX, D), D_MIX ** -0.5),
        'norm2_g': 1.0 + nrm(ks[9], (L, D), 0.01),
        'router_g_w': nrm(ks[10], (L, D, N_GROUPS), D ** -0.5),
        'router_g_b': nrm(ks[11], (L, N_GROUPS), 0.01),
        'router_e_w': nrm(ks[12], (L, D, N_EXPERTS), D ** -0.5),
        'router_e_b': nrm(ks[13], (L, N_EXPERTS), 0.01),
        'w_gate': nrm(ks[14], (L, N_EXPERTS, D, D_EXPERT), D ** -0.5),
        'w_up': nrm(ks[15], (L, N_EXPERTS, D, D_EXPERT), D ** -0.5),
        'w_down': nrm(ks[16], (L, N_EXPERTS, D_EXPERT, D), D_EXPERT ** -0.5),
        'final_g': 1.0 + nrm(ks[17], (D,), 0.01),
    }

def reference(x, norm1_g, w_in, conv_a_w, conv_c_w, conv_c_b, ln_c_g, ln_c_b, w_out,
              norm2_g, router_g_w, router_g_b, router_e_w, router_e_b,
              w_gate, w_up, w_down, final_g):
    splits = [3 * D_CONV, 3 * D_CONV + D_ATT, 3 * D_CONV + 2 * D_ATT,
              3 * D_CONV + 3 * D_ATT]
    for l in range(DEPTH):
        h = rmsnorm(x, norm1_g[l])
        u = h @ w_in[l]
        u_a, u_q, u_k, u_v, u_c = jnp.split(u, splits, axis=-1)
        y_a = short_conv_mixer(u_a, conv_a_w[l])
        y_b = moba_attention(u_q, u_k, u_v)
        y_c = conformer_conv_mixer(u_c, conv_c_w[l], conv_c_b[l], ln_c_g[l], ln_c_b[l])
        x = x + jnp.concatenate([y_a, y_b, y_c], axis=-1) @ w_out[l]
        h = rmsnorm(x, norm2_g[l])
        x = x + hierarchical_moe(h, router_g_w[l], router_g_b[l], router_e_w[l], router_e_b[l],
                                 w_gate[l], w_up[l], w_down[l])
    return rmsnorm(x, final_g)


_drawn_inputs = setup_inputs


def setup_inputs(seed=0):
    import zlib

    import numpy as np

    out = dict(_drawn_inputs(seed))
    spreads = {}
    factors = {'norm1_g': 2.909,
     'conv_c_b': 3.441,
     'ln_c_g': 14.004,
     'ln_c_b': 49.054,
     'norm2_g': 3.218,
     'router_g_b': 8.883,
     'router_e_b': 19.693,
     'final_g': 180.779}
    for name, (base, spread) in spreads.items():
        noise = np.random.default_rng([zlib.crc32(name.encode()), seed]).standard_normal(out[name].shape)
        drawn = base * np.exp(spread * noise) if base else spread * noise
        out[name] = __import__('jax').numpy.asarray(drawn.astype(out[name].dtype))
    for name, factor in factors.items():
        out[name] = (out[name] * factor).astype(out[name].dtype)
    return out
```

```python
from contextlib import ExitStack

import concourse.bass as bass
from concourse import mybir

ALU = mybir.AluOpType
ACT = mybir.ActivationFunctionType
AX = mybir.AxisListType
F32 = mybir.dt.float32
I32 = mybir.dt.int32
U32 = mybir.dt.uint32

P = 128
S = 256
T = S // P
D = 2048
C = D // P
NB = 512
J = NB // P
N_HEADS = 8
HALF_HEADS = 4
TAPS_A, TAPS_C = 3, 31
GROUPS, PER_GROUP = 4, 8
E = GROUPS * PER_GROUP
SLOTS = 2 * S
OVER = 3
EPS = 1e-6
RING = 3
MASKED = -3.0e33

COL_BG, COL_CG, COL_XV, COL_Q, COL_K, COL_V, COL_A, COL_GATE = 0, 512, 1024, 1536, 2560, 3584, 4608, 5120
FIRST_BLOCKS = [COL_A, COL_GATE, COL_BG, COL_CG, COL_XV]
N_FIRST = len(FIRST_BLOCKS)
N_HALVES = N_HEADS // HALF_HEADS
OUT_BLOCK0 = N_FIRST + 3 * N_HALVES
MOE_BLOCK0 = OUT_BLOCK0 + D // NB
assert MOE_BLOCK0 % RING == 0
MOE_N = MOE_BLOCK0 // RING

R_WA, R_WC = 0, TAPS_A
R_CB = R_WC + TAPS_C
R_LG, R_LB = R_CB + 1, R_CB + 2
N_PAR = R_LB + 1


def hybrid_moe_program(nc, a, out, y_sorted):
    with ExitStack() as ctx:
        def sb(name, shape, dt=F32):
            return ctx.enter_context(nc.sbuf_tensor(name, shape, dt))

        def sem(name):
            return ctx.enter_context(nc.semaphore(name))

        ring = [sb(f"weight_slot{s}", [P, C * NB]) for s in range(RING)]
        x_tok = sb("x_tok", [P, T, D])
        zone_h = sb("zone_h", [P, C * S])
        zone_y = sb("zone_y", [P, C * S])
        ZC = 256 + TAPS_A - 1
        HCW = 256 + TAPS_C - 1
        Q0, K0, V0 = 0, HALF_HEADS * S, 2 * HALF_HEADS * S
        BG0 = V0 + T * NB
        Z0 = BG0 + J * S
        CV0 = Z0 + J * ZC
        HC0 = CV0 + J * S
        CG0 = HC0 + J * HCW
        A0 = CG0 + J * S
        XG_W = C * SLOTS + P
        zone_u = sb("zone_u", [P, max(A0 + J * S, XG_W)])

        hT = zone_h[:, :].rearrange("p (c s) -> p c s", c=C)
        h_tok = zone_y[:, :].rearrange("p (t d) -> p t d", t=T)
        h_tok_c = zone_y[:, :].rearrange("p (t k c) -> p t c k", t=T, c=C)
        yT = zone_y[:, :].rearrange("p (c s) -> p c s", c=C)
        qT = zone_u[:, Q0:Q0 + HALF_HEADS * S].rearrange("p (h s) -> p h s", h=HALF_HEADS)
        kT = zone_u[:, K0:K0 + HALF_HEADS * S].rearrange("p (h s) -> p h s", h=HALF_HEADS)
        v_tok = zone_u[:, V0:V0 + T * NB].rearrange("p (t n) -> p t n", t=T)
        bgT = zone_u[:, BG0:BG0 + J * S].rearrange("p (j s) -> p j s", j=J)
        zT = zone_u[:, Z0:Z0 + J * ZC].rearrange("p (j s) -> p j s", j=J)
        cvT = zone_u[:, CV0:CV0 + J * S].rearrange("p (j s) -> p j s", j=J)
        hcT = zone_u[:, HC0:HC0 + J * HCW].rearrange("p (j s) -> p j s", j=J)
        cgT = zone_u[:, CG0:CG0 + J * S].rearrange("p (j s) -> p j s", j=J)
        aT = zone_u[:, A0:A0 + J * S].rearrange("p (j s) -> p j s", j=J)
        sqT = cgT
        x_sorted = zone_u[:, 0:C * SLOTS].rearrange("p (c n) -> p c n", c=C)
        x_sorted_pad = zone_u[:, C * SLOTS:XG_W]
        x_win = zone_y[:, 0:C * P].rearrange("p (c n) -> p c n", c=C)
        pick = zone_h[:, 0:T * SLOTS].rearrange("p (t n) -> p t n", t=T)
        y_rows = zone_h[:, 0:D]
        silu_g = zone_h[:, D:D + NB]
        hidden = zone_h[:, D + NB:D + 2 * NB]
        hiddenT = zone_h[:, D + 2 * NB:D + 3 * NB].rearrange("p (j n) -> p j n", j=J)

        ident = sb("ident", [P, P])
        ones = sb("ones", [P, P])
        mean_w = sb("mean_w", [P, P])
        before = sb("before", [P, P])
        bias_d = sb("bias_d", [P, 3 * P])
        logits = sb("logits", [P, 2, 3 * P])
        probs = sb("probs", [P, 2, 3 * P])
        probsT = sb("probsT", [P, 3 * P])
        sigT = sb("sigT", [P, 2, S])
        rstdT = sb("rstdT", [P, S])
        par = sb("par", [N_PAR, NB])
        parT = sb("parT", [P, J, N_PAR])
        g1 = sb("g1", [P, C])
        g2 = sb("g2", [P, C])
        rg = sb("rg", [P, C * GROUPS])
        re = sb("re", [P, C * E])
        rbias = sb("rbias", [1, GROUPS + E])
        small = sb("small", [P, 64])
        lg = sb("lg", [P, T, GROUPS + E])
        r4 = sb("r4", [P, 4, T, GROUPS])
        r8 = sb("r8", [P, 6, T, PER_GROUP])
        r32 = sb("r32", [P, 4, T, E])
        chosen = sb("chosen", [P, 3, T, E])
        cntT = sb("cntT", [E, P])
        starts = sb("starts", [P, E + OVER + 1])
        counts = sb("counts", [P, E + OVER])
        over = sb("over", [P, 4, E])
        row_of = sb("row_of", [P, E + OVER])
        ramp = sb("ramp", [P, E])
        iota_row = logits[:, :, :].rearrange("p a b -> p (a b)")[:, 0:SLOTS]
        iota_p = sb("iota_p", [P, 1])
        start_i = sb("start_i", [1, E + OVER + 1], I32)
        over_i = sb("over_i", [1, 2 * OVER], I32)
        row_i = sb("row_i", [P, E + OVER], I32)
        row_now = sb("row_now", [P, 1], I32)
        slot_i = sb("slot_i", [P, 2 * T], I32)

        bank = [ctx.enter_context(nc.psum_tensor(f"bank{i}", [P, NB], F32)) for i in range(8)]

        x_loaded = [sem(f"x_loaded{t}") for t in range(T)]
        par_loaded = sem("par_loaded")
        router_loaded = sem("router_loaded")
        w_loaded = [sem(f"w_loaded{s}") for s in range(RING)]
        consts = sem("consts")
        pool_step = sem("pool_step")
        par_turned = sem("par_turned")
        par_ready = sem("par_ready")
        sum_sq = sem("sum_sq")
        mean_sq = sem("mean_sq")
        root = sem("root")
        h_ready = sem("h_ready")
        turned = sem("turned")
        turned_dve = sem("turned_dve")
        turned_act = sem("turned_act")
        proj = sem("proj")
        proj_act = sem("proj_act")
        proj_dve = sem("proj_dve")
        gate_sig = sem("gate_sig")
        conv_in = sem("conv_in")
        dve_step = sem("dve_step")
        act_step = sem("act_step")
        conv_tap = sem("conv_tap")
        conv_done = sem("conv_done")
        ln_mean = sem("ln_mean")
        ln_centred = sem("ln_centred")
        ln_square = sem("ln_square")
        ln_var = sem("ln_var")
        ln_eps = sem("ln_eps")
        ln_root = sem("ln_root")
        ln_scaled = sem("ln_scaled")
        ya_ready = sem("ya_ready")
        yc_ready = sem("yc_ready")
        scores = sem("scores")
        att_step = sem("att_step")
        neg_max = sem("neg_max")
        exps = sem("exps")
        probs_ready = sem("probs_ready")
        probs_turned = sem("probs_turned")
        probsT_ready = sem("probsT_ready")
        att_out = sem("att_out")
        att_copied = sem("att_copied")
        mixed = sem("mixed")
        mixed_added = sem("mixed_added")
        routed = sem("routed")
        rt = sem("rt")
        rt_in = sem("rt_in")
        chosen_ready = sem("chosen_ready")
        cnt_done = sem("cnt_done")
        cnt_copied = sem("cnt_copied")
        pos_done = sem("pos_done")
        pick_ready = sem("pick_ready")
        sorted_done = sem("sorted_done")
        sorted_dve = sem("sorted_dve")
        sorted_act = sem("sorted_act")
        tables_ready = sem("tables_ready")
        win_ready = sem("win_ready")
        gate_done = sem("gate_done")
        up_done = sem("up_done")
        silu_done = sem("silu_done")
        hidden_ready = sem("hidden_ready")
        hidden_turned = sem("hidden_turned")
        hiddenT_ready = sem("hiddenT_ready")
        down_done = sem("down_done")
        y_act = sem("y_act")
        y_dve = sem("y_dve")
        row_ready = sem("row_ready")
        y_stored = sem("y_stored")
        store_started = sem("store_started")
        rows_free = sem("rows_free")
        fg_loaded = sem("fg_loaded")
        slot_ready = sem("slot_ready")
        gathered = [sem(f"gathered{t}") for t in range(T)]
        rows_done = sem("rows_done")
        fin_ms = sem("fin_ms")
        fin_root = sem("fin_root")
        fin_ready = sem("fin_ready")
        stored = sem("stored")

        def col(i, n=1):
            return small[:, i:i + n]

        SS, MS, RT_, RSTD = col(0, 2), col(2, 2), col(4, 2), col(6, 2)
        NMAX, ESUM, ERCP = small[:, 8:12], small[:, 12:16], small[:, 16:20]
        GM, GS, GR, PGRP, KM4 = (col(20 + 2 * i, 2) for i in range(5))
        EM, ES, ER, Q1, Q2, KM8 = (col(30 + 2 * i, 2) for i in range(6))
        GATE1, GATE2, TOP = col(42, 2), col(44, 2), col(46, 2)
        SLOT = small[:, 48:52]
        KOV, NONE = small[:, 52:55], small[:, 55:58]

        FIRST_CONSTS, CONSTS = 5, 10

        w_in = a["w_in"][0].rearrange("(p c) n -> p c n", c=C)
        w_out = a["w_out"][0].rearrange("(c p) n -> p c n", p=P)

        def slot3(s):
            return ring[s][:, :].rearrange("p (c n) -> p c n", c=C)

        def load_block(sp, n, src):
            sp.dma_start(slot3(n % RING), src).then_inc(w_loaded[n % RING], 16)

        def expert_weights(e):
            gate = a["w_gate"][0][bass.ds(e, 1)].rearrange("e (p c) n -> p (e c n)", c=C)
            up = a["w_up"][0][bass.ds(e, 1)].rearrange("e (p c) n -> p (e c n)", c=C)
            down = a["w_down"][0][bass.ds(e, 1)].rearrange("e (p j) n -> p (e j n)", j=J)
            return gate, up, down

        def load_expert(sp, e, which, t):
            if which == 0:
                sp.wait_ge(gate_done, t)
            elif which == 1:
                sp.wait_ge(up_done, t)
            else:
                sp.wait_ge(down_done, t * (D // NB))
            start_expert(sp, e, which)

        def start_expert(sp, e, which):
            sp.dma_start(ring[which][:, :], expert_weights(e)[which]).then_inc(w_loaded[which], 16)

        block = ctx.enter_context(nc.Block())

        @block.sync
        def _(sp):
            for t in range(T):
                sp.dma_start(x_tok[:, t, :], a["x"][0, t * P:(t + 1) * P, :]).then_inc(x_loaded[t], 16)
            for n, c0 in enumerate(FIRST_BLOCKS):
                if n >= RING:
                    sp.wait_ge(proj, J * (n - RING + 1))
                load_block(sp, n, w_in[:, :, c0:c0 + NB])
            with sp.Fori(0, N_HALVES) as f:
                for m, (c0, units, per_half) in enumerate(((COL_Q, 3 * J, 12), (COL_K, 4 * J, 12), (COL_V, 5 * J, 10))):
                    s = (N_FIRST + m) % RING
                    sp.wait_ge(proj, f * per_half + units)
                    sp.dma_start(slot3(s), w_in[:, :, bass.ds(f * NB + c0, NB)]).then_inc(w_loaded[s], 16)
            for b in range(D // NB):
                if b < RING:
                    sp.wait_ge(proj, (34, 38, 40)[b])
                else:
                    sp.wait_ge(mixed, 2)
                load_block(sp, OUT_BLOCK0 + b, w_out[:, :, b * NB:(b + 1) * NB])
            sp.wait_ge(mixed, 4)
            start_expert(sp, 0, 0)
            sp.wait_ge(mixed, 6)
            start_expert(sp, 0, 1)
            load_expert(sp, 1, 0, 1)
            load_expert(sp, 1, 1, 1)
            sp.wait_ge(mixed, 8)
            start_expert(sp, 0, 2)
            with sp.Fori(1, E - 1) as e:
                load_expert(sp, e + 1, 0, e + 1)
                load_expert(sp, e + 1, 1, e + 1)
                load_expert(sp, e, 2, e)
            load_expert(sp, E - 1, 2, E - 1)
            sp.wait_ge(tables_ready, 1)
            flag = sp.value_load(over_i[0:1, OVER:OVER + 1], min_val=0, max_val=E)
            with sp.If(flag > 0):
                with sp.Fori(0, OVER) as i:
                    e = sp.value_load(over_i[0:1, bass.ds(i, 1)], min_val=0, max_val=E - 1)
                    for which in range(3):
                        load_expert(sp, e, which, i + E)
            sp.wait_ge(rows_done, 1)
            sp.dma_start(ring[1][:, 0:D], a["final_g"].rearrange("(o d) -> o d", o=1).broadcast_to([P, D])).then_inc(fg_loaded, 16)
            for t in range(T):
                sp.wait_ge(fin_ready, t + 1)
                sp.dma_start(out[t * P:(t + 1) * P, :], x_tok[:, t, :]).then_inc(stored, 16)
            sp.wait_ge(stored, 16 * T)

        @block.gpsimd
        def _(pool):
            step = [0]

            def link(ins):
                step[0] += 1
                ins.then_inc(pool_step, 1)
                pool.wait_ge(pool_step, step[0])

            pool.sem_inc(rows_free, 1)

            pool.memset(zT[:, :, 0:TAPS_A - 1], 0.0).then_inc(consts, 1)
            pool.memset(hcT[:, :, 0:TAPS_C - 1], 0.0).then_inc(consts, 1)
            pool.memset(ones[:, :], 1.0).then_inc(consts, 1)
            pool.memset(mean_w[:, :], 1.0 / NB).then_inc(consts, 1)
            link(pool.memset(ident[:, :], 0.0))
            pool.affine_select(out=ident[:, :], in_=ident[:, :], compare_op=ALU.not_equal, fill=1.0,
                               base=0, pattern=[[-1, P]], channel_multiplier=1).then_inc(consts, 1)
            pool.iota(bias_d[:, 0:P], pattern=[[1, P]], base=0, channel_multiplier=-1,
                      allow_small_or_imprecise_dtypes=True)
            link(pool.iota(bias_d[:, P:3 * P], pattern=[[1, 2 * P]], base=-P, channel_multiplier=-1,
                           allow_small_or_imprecise_dtypes=True))
            pool.affine_select(out=bias_d[:, 0:P], in_=bias_d[:, 0:P], compare_op=ALU.is_ge, fill=MASKED,
                               base=0, pattern=[[-1, P]], channel_multiplier=1).then_inc(consts, 1)
            pool.affine_select(out=bias_d[:, P:3 * P], in_=bias_d[:, P:3 * P], compare_op=ALU.is_ge, fill=MASKED,
                               base=P, pattern=[[-1, 2 * P]], channel_multiplier=1).then_inc(consts, 1)
            link(pool.memset(before[:, :], 1.0))
            pool.affine_select(out=before[:, :], in_=before[:, :], compare_op=ALU.is_ge, fill=0.0,
                               base=-1, pattern=[[1, P]], channel_multiplier=-1).then_inc(consts, 1)
            pool.iota(ramp[:, :], pattern=[[-1, E]], base=E, channel_multiplier=0,
                      allow_small_or_imprecise_dtypes=True).then_inc(consts, 1)
            pool.iota(iota_p[:, :], pattern=[[1, 1]], base=0, channel_multiplier=1,
                      allow_small_or_imprecise_dtypes=True).then_inc(consts, 1)
            pool.wait_ge(probs_ready, N_HEADS)
            pool.iota(iota_row, pattern=[[1, SLOTS]], base=0, channel_multiplier=0,
                      allow_small_or_imprecise_dtypes=True).then_inc(consts, 1)

            def store_rows(t):
                pool.wait_ge(y_act, 2 * t + 4)
                pool.wait_ge(y_dve, 2 * t + 4)
                pool.wait_ge(row_ready, t + 1)
                pool.sem_inc(store_started, 1)
                pool.indirect_dma_start(
                    out=y_sorted, out_offset=bass.IndirectOffsetOnAxis(ap=row_now[:, 0:1], axis=0),
                    in_=y_rows, in_offset=None, bounds_check=SLOTS - 1, oob_is_err=False).then_inc(y_stored, 16)
                pool.wait_ge(y_stored, 16 * t + 16)
                pool.sem_inc(rows_free, 1)

            pool.wait_ge(tables_ready, 1)
            with pool.Fori(0, E) as e:
                store_rows(e)
            flag = pool.value_load(over_i[0:1, OVER:OVER + 1], min_val=0, max_val=E)
            with pool.If(flag > 0):
                with pool.Fori(E, E + OVER) as t:
                    store_rows(t)
            pool.sem_inc(rows_done, 1)
            for t in range(T):
                for k in range(2):
                    pool.indirect_dma_start(
                        out=ring[2 * k][:, t * D:(t + 1) * D], out_offset=None, in_=y_sorted,
                        in_offset=bass.IndirectOffsetOnAxis(ap=slot_i[:, k * T + t:k * T + t + 1], axis=0),
                        bounds_check=SLOTS - 1, oob_is_err=True).then_inc(gathered[t], 16)

        @block.scalar
        def _(act):
            step = [0]

            def link(ins):
                step[0] += 1
                ins.then_inc(act_step, 1)
                act.wait_ge(act_step, step[0])

            for row, src in ((R_WA, a["conv_a_w"][0]), (R_WC, a["conv_c_w"][0]), (R_CB, a["conv_c_b"]),
                             (R_LG, a["ln_c_g"]), (R_LB, a["ln_c_b"])):
                act.dma_start(par[row:row + src.shape[0], :], src).then_inc(par_loaded, 16)
            act.dma_start(g1[:, :], a["norm1_g"][0].rearrange("(p c) -> p c", c=C)).then_inc(par_loaded, 16)
            act.dma_start(g2[:, :], a["norm2_g"][0].rearrange("(p c) -> p c", c=C)).then_inc(router_loaded, 16)
            act.dma_start(rg[:, :], a["router_g_w"][0].rearrange("(p c) g -> p (c g)", c=C)).then_inc(router_loaded, 16)
            act.dma_start(re[:, :], a["router_e_w"][0].rearrange("(p c) g -> p (c g)", c=C)).then_inc(router_loaded, 16)
            act.dma_start(rbias[:, 0:GROUPS], a["router_g_b"]).then_inc(router_loaded, 16)
            act.dma_start(rbias[:, GROUPS:], a["router_e_b"]).then_inc(router_loaded, 16)

            for t in range(T):
                act.wait_ge(x_loaded[t], 16)
                nc.scalar.activation(h_tok[:, t, :], x_tok[:, t, :], ACT.Square, accum_out=SS[:, t:t + 1]).then_inc(sum_sq, 1)
            act.wait_ge(mean_sq, 1)
            nc.scalar.activation(RT_, MS, ACT.Sqrt).then_inc(root, 1)

            def turned_chunks(gain, base):
                for k in range(1, C // 2, 2):
                    act.wait_ge(turned, base + k + 1)
                    for i in range(2):
                        nc.scalar.activation(hT[:, 2 * k + i, :], bank[k % 4][:, i * S:(i + 1) * S], ACT.Copy,
                                             scale=gain[:, 2 * k + i:2 * k + i + 1]).then_inc(turned_act, 1)

            act.wait_ge(par_loaded, 16 * 6)
            turned_chunks(g1, 0)

            for n in range(4 * J):
                j = n % J
                act.wait_ge(proj, n + 1)
                src = bank[n % 4][:, 0:S]
                if n < J:
                    nc.scalar.activation(aT[:, j, :], src, ACT.Copy).then_inc(proj_act, 1)
                elif n < 2 * J:
                    if j >= 2:
                        act.wait_ge(conv_in, j - 1)
                    nc.scalar.activation(sigT[:, j % 2, :], src, ACT.Sigmoid).then_inc(proj_act, 1)
                else:
                    dst = bgT if n < 3 * J else cgT
                    nc.scalar.activation(dst[:, j, :], src, ACT.Copy).then_inc(proj_act, 1)

            for j in range(J):
                act.wait_ge(ln_centred, j + 1)
                nc.scalar.activation(sqT[:, j, :], cvT[:, j, :], ACT.Square).then_inc(ln_square, 1)
            act.wait_ge(ln_eps, 1)
            nc.scalar.activation(rstdT[:, :], sigT[:, 0, :], ACT.Sqrt).then_inc(ln_root, 1)
            for j in range(J):
                act.wait_ge(ln_scaled, j + 1)
                nc.scalar.activation(yT[:, 3 * J + j, :], cvT[:, j, :], ACT.Silu, bias=parT[:, j, R_LB:R_LB + 1],
                                     scale=parT[:, j, R_LG:R_LG + 1]).then_inc(yc_ready, 1)

            with act.Fori(0, N_HALVES) as f:
                base = f * 10
                for m in range(10):
                    act.wait_ge(proj, base + (5 * J + m + 1))
                    if m < 2 * J:
                        src, j = bank[m % 4][:, 0:S], m % J
                        if m < J:
                            nc.scalar.activation(qT[:, j, :], src, ACT.Copy, scale=float(P) ** -0.5).then_inc(proj_act, 1)
                        else:
                            nc.scalar.activation(kT[:, j, :], src, ACT.Copy).then_inc(proj_act, 1)
                    else:
                        nc.scalar.activation(v_tok[:, m - 2 * J, :], bank[m % 4][:, :], ACT.Copy).then_inc(proj_act, 1)
                for h in range(HALF_HEADS):
                    b = h % 2
                    act.wait_ge(neg_max, f * HALF_HEADS + (h + 1))
                    for lo, hi, i in ((0, P, 0), (P, 3 * P, 1)):
                        ins = nc.scalar.activation(probs[:, b, lo:hi], logits[:, b, lo:hi], ACT.Exp,
                                                   bias=NMAX[:, 2 * b + i:2 * b + i + 1],
                                                   accum_out=ESUM[:, 2 * b + i:2 * b + i + 1])
                        ins.then_inc(exps, 1)
                    act.wait_ge(probs_turned, f * HALF_HEADS + (h + 1))
                    nc.scalar.activation(probsT[:, :], bank[6][:, 0:3 * P], ACT.Copy).then_inc(probsT_ready, 1)
                    act.wait_ge(att_out, f * HALF_HEADS + (h + 1))
                    nc.scalar.activation(yT[:, bass.ds(f * HALF_HEADS + (J + h), 1), :].rearrange("p a s -> p (a s)"),
                                         bank[7][:, 0:S], ACT.Copy).then_inc(att_copied, 1)

            for t in range(T):
                act.wait_ge(mixed_added, 2 * (D // NB) - T + t + 1)
                nc.scalar.activation(zone_u[:, t * D:(t + 1) * D], x_tok[:, t, :], ACT.Square, accum_out=SS[:, t:t + 1]).then_inc(sum_sq, 1)
            act.wait_ge(mean_sq, 2)
            nc.scalar.activation(RT_, MS, ACT.Sqrt).then_inc(root, 1)
            act.wait_ge(router_loaded, 16 * 5)
            turned_chunks(g2, C // 2)

            act.wait_ge(rt_in, 1)
            nc.scalar.activation(r4[:, 1], r4[:, 0], ACT.Exp).then_inc(rt, 1)
            act.wait_ge(rt_in, 2)
            nc.scalar.activation(r8[:, 1], r8[:, 0], ACT.Exp).then_inc(rt, 1)
            act.wait_ge(cnt_done, 1)
            nc.scalar.activation(cntT[:, :], bank[5][0:E, 0:P], ACT.Copy).then_inc(cnt_copied, 1)
            for c in range(1, C, 2):
                act.wait_ge(sorted_done, c + 1)
                nc.scalar.activation(x_sorted[:, c, :], bank[c % 4][:, :], ACT.Copy,
                                     scale=g2[:, c:c + 1]).then_inc(sorted_act, 1)

            def silu_of(t):
                act.wait_ge(gate_done, t + 1)
                act.wait_ge(tables_ready, 1)
                nc.scalar.activation(silu_g, bank[0][:, :], ACT.Silu).then_inc(silu_done, 1)

            def rows_out(t):
                for i in range(2):
                    act.wait_ge(down_done, 4 * t + i + 1)
                    if i == 0:
                        act.wait_ge(rows_free, t + 1)
                    nc.scalar.activation(y_rows[:, i * NB:(i + 1) * NB], bank[4 + i][:, :], ACT.Copy).then_inc(y_act, 1)

            act.sem_inc(y_act, 2)
            silu_of(0)
            with act.Fori(1, E) as e:
                act.wait_ge(hidden_ready, e)
                silu_of(e)
                rows_out(e - 1)
            rows_out(E - 1)
            flag = act.value_load(over_i[0:1, OVER:OVER + 1], min_val=0, max_val=E)
            with act.If(flag > 0):
                with act.Fori(E, E + OVER) as t:
                    act.wait_ge(hidden_ready, t)
                    silu_of(t)
                    rows_out(t)
            for t in range(T):
                act.wait_ge(fin_ms, 2 * t + 1)
                nc.scalar.activation(h_tok[:, t, :], x_tok[:, t, :], ACT.Square, accum_out=SS[:, t:t + 1]).then_inc(fin_root, 1)
                act.wait_ge(fin_ms, 2 * t + 2)
                nc.scalar.activation(RT_[:, t:t + 1], MS[:, t:t + 1], ACT.Sqrt).then_inc(fin_root, 1)

        @block.vector
        def _(dve):
            step = [0]

            def link(ins):
                step[0] += 1
                ins.then_inc(dve_step, 1)
                dve.wait_ge(dve_step, step[0])

            V = nc.vector

            def rstd_of(n):
                dve.wait_ge(sum_sq, 2 * n)
                V.tensor_scalar(MS, SS, 1.0 / D, EPS, ALU.mult, ALU.add).then_inc(mean_sq, 1)
                dve.wait_ge(root, n)
                link(V.reciprocal(RSTD, RT_))

            def turned_chunks(gain, base):
                for k in range(0, C // 2, 2):
                    dve.wait_ge(turned, base + k + 1)
                    for i in range(2):
                        V.tensor_scalar(hT[:, 2 * k + i, :], bank[k % 4][:, i * S:(i + 1) * S],
                                        gain[:, 2 * k + i:2 * k + i + 1], None, ALU.mult).then_inc(turned_dve, 1)

            rstd_of(1)
            for t in range(T):
                V.tensor_scalar(h_tok[:, t, :], x_tok[:, t, :], RSTD[:, t:t + 1], None, ALU.mult).then_inc(h_ready, 1)
            dve.wait_ge(par_turned, 1)
            V.tensor_copy(parT[:, :, :], bank[7][:, 0:J * N_PAR].rearrange("p (j n) -> p j n", j=J)).then_inc(par_ready, 1)
            dve.wait_ge(par_loaded, 16 * 6)
            turned_chunks(g1, 0)

            for j in range(J):
                dve.wait_ge(proj_act, J + j + 1)
                if j == 0:
                    dve.wait_ge(consts, FIRST_CONSTS)
                V.tensor_tensor(hcT[:, j, TAPS_C - 1:HCW], aT[:, j, :], sigT[:, j % 2, :], ALU.mult).then_inc(conv_in, 1)
            dve.wait_ge(par_ready, 1)
            dve.wait_ge(conv_in, J)
            for j in range(J):
                V.tensor_scalar(cvT[:, j, :], hcT[:, j, 0:S], parT[:, j, R_WC:R_WC + 1], parT[:, j, R_CB:R_CB + 1],
                                ALU.mult, ALU.add).then_inc(conv_tap, 1)
            with dve.Fori(1, TAPS_C) as i:
                for j in range(J):
                    dve.wait_ge(conv_tap, i * J + (j + 1 - J))
                    V.scalar_tensor_tensor(cvT[:, j, :], hcT[:, j, bass.ds(i, S)], parT[:, j, bass.ds(i + R_WC, 1)],
                                           cvT[:, j, :], ALU.mult, ALU.add).then_inc(conv_tap, 1)
            dve.wait_ge(conv_tap, TAPS_C * J)
            V.engine_nop().then_inc(conv_done, 1)

            for j in range(J):
                dve.wait_ge(proj, 4 * J + j + 1)
                dve.wait_ge(proj_act, 3 * J + j + 1)
                V.tensor_tensor(zT[:, j, TAPS_A - 1:ZC], cgT[:, j, :], bank[j % 4][:, 0:S], ALU.mult).then_inc(proj_dve, 1)
            for j in range(J):
                dve.wait_ge(ln_mean, 1)
                V.tensor_tensor(cvT[:, j, :], cvT[:, j, :], bank[4][:, 0:S], ALU.subtract).then_inc(ln_centred, 1)
            dve.wait_ge(proj_dve, J)
            for j in range(J):
                link(V.tensor_scalar(aT[:, j, :], zT[:, j, 0:S], parT[:, j, R_WA:R_WA + 1], None, ALU.mult))
                for i in range(1, TAPS_A):
                    link(V.scalar_tensor_tensor(aT[:, j, :], zT[:, j, i:i + S], parT[:, j, R_WA + i:R_WA + i + 1],
                                                aT[:, j, :], ALU.mult, ALU.add))
                V.tensor_tensor(yT[:, j, :], bgT[:, j, :], aT[:, j, :], ALU.mult).then_inc(ya_ready, 1)
            dve.wait_ge(ln_var, 1)
            V.tensor_scalar(sigT[:, 0, :], bank[5][:, 0:S], EPS, None, ALU.add).then_inc(ln_eps, 1)
            dve.wait_ge(ln_root, 1)
            link(V.reciprocal(rstdT[:, :], rstdT[:, :]))
            for j in range(J):
                V.tensor_tensor(cvT[:, j, :], cvT[:, j, :], rstdT[:, :], ALU.mult).then_inc(ln_scaled, 1)

            dve.wait_ge(consts, CONSTS)
            with dve.Fori(0, N_HALVES) as f:
                A_STEPS = 3 * HALF_HEADS + 1

                def att(ins, k):
                    ins.then_inc(att_step, 1)
                    dve.wait_ge(att_step, f * A_STEPS + k)

                k = 0
                for h in range(HALF_HEADS):
                    b = h % 2
                    dve.wait_ge(scores, f * HALF_HEADS + (h + 1))
                    k += 1
                    att(V.scalar_tensor_tensor(logits[:, b, :], bias_d[:, :], 0.5 ** (h + 1), bank[4 + b][:, 0:3 * P],
                                               ALU.mult, ALU.add), k)
                    V.tensor_reduce(GM[:, 0:1], logits[:, b, 0:P], AX.X, ALU.max)
                    k += 1
                    att(V.tensor_reduce(GM[:, 1:2], logits[:, b, P:3 * P], AX.X, ALU.max), k)
                    V.tensor_scalar(NMAX[:, 2 * b:2 * b + 2], GM, -1.0, None, ALU.mult).then_inc(neg_max, 1)
                    dve.wait_ge(exps, f * (2 * HALF_HEADS) + (2 * h + 2))
                    k += 1
                    att(V.reciprocal(ERCP[:, 2 * b:2 * b + 2], ESUM[:, 2 * b:2 * b + 2]), k)
                    V.tensor_scalar(probs[:, b, 0:P], probs[:, b, 0:P], ERCP[:, 2 * b:2 * b + 1], None, ALU.mult)
                    V.tensor_scalar(probs[:, b, P:3 * P], probs[:, b, P:3 * P], ERCP[:, 2 * b + 1:2 * b + 2], None,
                                    ALU.mult).then_inc(probs_ready, 1)
                k += 1
                att(V.tensor_scalar(bias_d[:, :], bias_d[:, :], 0.5 ** HALF_HEADS, None, ALU.mult), k)

            for u in range(2 * (D // NB)):
                b, t = u // 2, u % 2
                dve.wait_ge(mixed, u + 1)
                V.tensor_tensor(x_tok[:, t, b * NB:(b + 1) * NB], x_tok[:, t, b * NB:(b + 1) * NB], bank[u % 4][:, :],
                                ALU.add).then_inc(mixed_added, 1)

            rstd_of(2)
            for t in range(T):
                V.tensor_scalar(h_tok[:, t, :], x_tok[:, t, :], RSTD[:, t:t + 1], None, ALU.mult).then_inc(h_ready, 1)
            dve.wait_ge(router_loaded, 16 * 5)
            turned_chunks(g2, C // 2)

            dve.wait_ge(routed, 1)
            link(V.tensor_copy(lg[:, :, :], bank[4][:, 0:T * (GROUPS + E)].rearrange("p (t n) -> p t n", t=T)))
            lgrp = lg[:, :, 0:GROUPS]

            def spread(v, n):
                return v.unsqueeze(2).broadcast_to([P, T, n])

            link(V.tensor_reduce(GM, lgrp, AX.X, ALU.max))
            V.tensor_tensor(r4[:, 0], lgrp, spread(GM, GROUPS), ALU.subtract).then_inc(rt_in, 1)
            dve.wait_ge(rt, 1)
            link(V.tensor_reduce(GS, r4[:, 1], AX.X, ALU.add))
            link(V.reciprocal(GR, GS))
            link(V.tensor_tensor(r4[:, 1], r4[:, 1], spread(GR, GROUPS), ALU.mult))
            link(V.tensor_reduce(PGRP, r4[:, 1], AX.X, ALU.max))

            def first_max(dst, vals, top, key, km, n):
                link(V.tensor_tensor(key, vals, spread(top, n), ALU.is_equal))
                link(V.tensor_tensor(key, key, ramp[:, E - n:E].unsqueeze(1).broadcast_to([P, T, n]), ALU.mult))
                link(V.tensor_reduce(km, key, AX.X, ALU.max))
                link(V.tensor_tensor(dst, key, spread(km, n), ALU.is_equal))

            first_max(r4[:, 3], r4[:, 1], PGRP, r4[:, 2], KM4, GROUPS)
            for t in range(T):
                link(V.tensor_tensor(r32[:, 0, t, :].rearrange("p (g e) -> p g e", g=GROUPS),
                                     lg[:, t, GROUPS:].rearrange("p (g e) -> p g e", g=GROUPS),
                                     r4[:, 3, t, :].unsqueeze(2).broadcast_to([P, GROUPS, PER_GROUP]), ALU.mult))
                link(V.tensor_reduce(r8[:, 2, t, :], r32[:, 0, t, :].rearrange("p (g e) -> p e g", g=GROUPS), AX.X, ALU.add))
            link(V.tensor_reduce(EM, r8[:, 2], AX.X, ALU.max))
            V.tensor_tensor(r8[:, 0], r8[:, 2], spread(EM, PER_GROUP), ALU.subtract).then_inc(rt_in, 1)
            dve.wait_ge(rt, 2)
            link(V.tensor_reduce(ES, r8[:, 1], AX.X, ALU.add))
            link(V.reciprocal(ER, ES))
            link(V.tensor_tensor(r8[:, 1], r8[:, 1], spread(ER, PER_GROUP), ALU.mult))
            link(V.tensor_reduce(Q1, r8[:, 1], AX.X, ALU.max))
            first_max(r8[:, 3], r8[:, 1], Q1, r8[:, 2], KM8, PER_GROUP)
            link(V.scalar_tensor_tensor(r8[:, 1], r8[:, 3], -2.0, r8[:, 1], ALU.mult, ALU.add))
            link(V.tensor_reduce(Q2, r8[:, 1], AX.X, ALU.max))
            first_max(r8[:, 4], r8[:, 1], Q2, r8[:, 2], KM8, PER_GROUP)
            link(V.tensor_tensor(TOP, Q1, Q2, ALU.add))
            link(V.reciprocal(TOP, TOP))
            link(V.tensor_tensor(GATE1, PGRP, Q1, ALU.mult))
            link(V.tensor_tensor(GATE1, GATE1, TOP, ALU.mult))
            link(V.tensor_tensor(GATE2, PGRP, Q2, ALU.mult))
            link(V.tensor_tensor(GATE2, GATE2, TOP, ALU.mult))
            for k in range(2):
                for t in range(T):
                    link(V.tensor_tensor(chosen[:, k, t, :].rearrange("p (g e) -> p g e", g=GROUPS),
                                         r4[:, 3, t, :].unsqueeze(2).broadcast_to([P, GROUPS, PER_GROUP]),
                                         r8[:, 3 + k, t, :].unsqueeze(1).broadcast_to([P, GROUPS, PER_GROUP]), ALU.mult))
            V.tensor_tensor(chosen[:, 2], chosen[:, 0], chosen[:, 1], ALU.add).then_inc(chosen_ready, 1)

            dve.wait_ge(pos_done, 1)
            posv = bank[4][:, 128:128 + T * E].rearrange("p (t e) -> p t e", t=T)
            for k in range(2):
                link(V.tensor_tensor(r32[:, k], chosen[:, k], posv, ALU.mult))
                link(V.tensor_reduce(SLOT[:, k * T:(k + 1) * T], r32[:, k], AX.X, ALU.add))
            dve.wait_ge(consts, CONSTS + 1)
            for t in range(T):
                link(V.tensor_scalar(pick[:, t, :], iota_row, SLOT[:, t:t + 1], None, ALU.is_equal))
                V.scalar_tensor_tensor(pick[:, t, :], iota_row, SLOT[:, T + t:T + t + 1], pick[:, t, :], ALU.is_equal,
                                       ALU.add).then_inc(pick_ready, 1)
            link(V.tensor_copy(slot_i[:, :], SLOT))
            link(V.memset(starts[:, E + OVER:], 0.0))
            link(V.tensor_copy(starts[:, 0:E], bank[4][:, 192:192 + E]))
            link(V.tensor_copy(counts[:, 0:E], bank[4][:, 224:224 + E]))
            V.memset(x_sorted_pad, 0.0)
            for c in range(0, C, 2):
                dve.wait_ge(sorted_done, c + 1)
                V.tensor_scalar(x_sorted[:, c, :], bank[c % 4][:, :], g2[:, c:c + 1], None, ALU.mult).then_inc(sorted_dve, 1)

            link(V.tensor_scalar(over[:, 0, :], counts[:, 0:E], float(P), None, ALU.is_gt))
            link(V.tensor_tensor(over[:, 0, :], over[:, 0, :], ramp[:, :], ALU.mult))
            link(V.tensor_scalar(over[:, 3, :], starts[:, 0:E], float(P), None, ALU.add))
            for i in range(OVER):
                link(V.tensor_reduce(KOV[:, i:i + 1], over[:, 0, :], AX.X, ALU.max))
                link(V.tensor_scalar(over[:, 1, :], ramp[:, :], KOV[:, i:i + 1], None, ALU.is_equal))
                link(V.tensor_tensor(over[:, 2, :], over[:, 1, :], over[:, 3, :], ALU.mult))
                link(V.tensor_reduce(starts[:, E + i:E + i + 1], over[:, 2, :], AX.X, ALU.add))
                link(V.tensor_tensor(over[:, 2, :], over[:, 1, :], counts[:, 0:E], ALU.mult))
                link(V.tensor_reduce(counts[:, E + i:E + i + 1], over[:, 2, :], AX.X, ALU.add))
                link(V.scalar_tensor_tensor(over[:, 0, :], over[:, 0, :], KOV[:, i:i + 1], over[:, 0, :],
                                            ALU.is_lt, ALU.mult))
            link(V.tensor_scalar(counts[:, E:], counts[:, E:], -float(P), None, ALU.add))
            link(V.tensor_scalar(row_of[:, :], counts[:, :], iota_p[:, 0:1], float(4 * SLOTS), ALU.is_le, ALU.mult))
            link(V.tensor_tensor(row_of[:, :], row_of[:, :], starts[:, 0:E + OVER], ALU.add))
            link(V.tensor_scalar(row_of[:, :], row_of[:, :], iota_p[:, 0:1], None, ALU.add))
            link(V.tensor_copy(row_i[:, :], row_of[:, :]))
            link(V.tensor_copy(start_i[:, :], starts[0:1, :]))
            link(V.tensor_scalar(NONE, KOV, -1.0, float(E), ALU.mult, ALU.add))
            link(V.tensor_scalar(NONE, NONE, float(E - 1), None, ALU.min))
            link(V.tensor_copy(over_i[:, 0:OVER], NONE[0:1, :]))
            link(V.tensor_copy(over_i[:, OVER:2 * OVER], KOV[0:1, :]))
            V.engine_nop().then_inc(tables_ready, 1)

            dve.wait_ge(sorted_act, C // 2)
            dve.wait_ge(sorted_dve, C // 2)

            def window(t):
                first = dve.value_load(start_i[0:1, bass.ds(t, 1)], min_val=0, max_val=SLOTS)
                V.tensor_copy(x_win[:, :, :], x_sorted_from(first)).then_inc(win_ready, 1)

            def x_sorted_from(first):
                return zone_u[:, bass.ds(first, C * SLOTS)].rearrange("p (c n) -> p c n", c=C)[:, :, 0:P]

            def hidden_of(t):
                dve.wait_ge(up_done, t + 1)
                dve.wait_ge(silu_done, t + 1)
                V.tensor_tensor(hidden, silu_g, bank[1][:, :], ALU.mult).then_inc(hidden_ready, 1)

            def turn_out(t):
                dve.wait_ge(hidden_turned, t + 1)
                V.tensor_copy(hiddenT, bank[2][:, :].rearrange("p (j n) -> p j n", j=J)).then_inc(hiddenT_ready, 1)

            def rows_out(t):
                dve.wait_ge(rows_free, t + 1)
                V.tensor_copy(row_now[:, :], row_i[:, bass.ds(t, 1)]).then_inc(row_ready, 1)
                for i in range(2, 4):
                    dve.wait_ge(down_done, 4 * t + i + 1)
                    V.tensor_copy(y_rows[:, i * NB:(i + 1) * NB], bank[4 + i][:, :]).then_inc(y_dve, 1)

            dve.sem_inc(y_dve, 2)
            window(0)
            hidden_of(0)
            window(1)
            with dve.Fori(1, E) as e:
                turn_out(e - 1)
                hidden_of(e)
                window(e + 1)
                rows_out(e - 1)
            turn_out(E - 1)
            rows_out(E - 1)
            flag = dve.value_load(over_i[0:1, OVER:OVER + 1], min_val=0, max_val=E)
            with dve.If(flag > 0):
                with dve.Fori(E, E + OVER) as t:
                    hidden_of(t)
                    turn_out(t)
                    rows_out(t)
                    window(t + 1)

            for t in range(T):
                dve.wait_ge(gathered[t], 32)
                link(V.scalar_tensor_tensor(x_tok[:, t, :], ring[0][:, t * D:(t + 1) * D], GATE1[:, t:t + 1],
                                            x_tok[:, t, :], ALU.mult, ALU.add))
                V.scalar_tensor_tensor(x_tok[:, t, :], ring[2][:, t * D:(t + 1) * D], GATE2[:, t:t + 1],
                                       x_tok[:, t, :], ALU.mult, ALU.add).then_inc(fin_ms, 1)
                dve.wait_ge(fin_root, 2 * t + 1)
                V.tensor_scalar(MS[:, t:t + 1], SS[:, t:t + 1], 1.0 / D, EPS, ALU.mult, ALU.add).then_inc(fin_ms, 1)
                dve.wait_ge(fin_root, 2 * t + 2)
                link(V.reciprocal(RSTD[:, t:t + 1], RT_[:, t:t + 1]))
                if t == 0:
                    dve.wait_ge(fg_loaded, 16)
                V.scalar_tensor_tensor(x_tok[:, t, :], x_tok[:, t, :], RSTD[:, t:t + 1], ring[1][:, 0:D],
                                       ALU.mult, ALU.mult).then_inc(fin_ready, 1)

        @block.tensor
        def _(pe):
            M = nc.tensor

            def turn_all(base):
                for k in range(C // 2):
                    if k >= 4:
                        pe.wait_ge(turned_act if k % 2 else turned_dve, base + 2 * ((k - 4) // 2 + 1))
                    for i in range(2):
                        for t in range(T):
                            ins = M.transpose(bank[k % 4][:, i * S + t * P:i * S + (t + 1) * P],
                                              h_tok_c[:, t, 2 * k + i, :], ident[:, :])
                    ins.then_inc(turned, 1)

            pe.wait_ge(consts, FIRST_CONSTS)
            pe.wait_ge(par_loaded, 16 * 6)
            for j in range(J):
                ins = M.transpose(bank[7][:, j * N_PAR:(j + 1) * N_PAR], par[:, j * P:(j + 1) * P], ident[0:N_PAR, 0:N_PAR])
            ins.then_inc(par_turned, 1)
            pe.wait_ge(h_ready, T)
            turn_all(0)
            pe.wait_ge(turned_dve, C // 2)
            pe.wait_ge(turned_act, C // 2)

            def channels(s, j, dst):
                w = slot3(s)
                for c in range(C):
                    ins = M.matmul(dst, w[:, c, j * P:(j + 1) * P], hT[:, c, :], start=(c == 0), stop=(c == C - 1))
                return ins

            for n in range(5 * J):
                b, j = n // J, n % J
                if j == 0:
                    pe.wait_ge(w_loaded[b % RING], 16 * (b // RING + 1))
                if n >= 4:
                    pe.wait_ge(proj_act, n - 3)
                ins = channels(b % RING, j, bank[n % 4][:, 0:S])
                ins.then_inc(proj, 1)
            pe.wait_ge(conv_done, 1)
            for j in range(J):
                ins = M.matmul(bank[4][:, 0:S], mean_w[:, :], cvT[:, j, :], start=(j == 0), stop=(j == J - 1))
            ins.then_inc(ln_mean, 1)
            for j in range(J):
                pe.wait_ge(ln_square, j + 1)
                ins = M.matmul(bank[5][:, 0:S], mean_w[:, :], sqT[:, j, :], start=(j == 0), stop=(j == J - 1))
            ins.then_inc(ln_var, 1)

            pe.wait_ge(proj_dve, J)
            pe.wait_ge(ln_eps, 1)
            with pe.Fori(0, N_HALVES) as f:
                for m in range(10):
                    blk = m // J
                    s = (N_FIRST + blk) % RING
                    if m % J == 0:
                        pe.wait_ge(w_loaded[s], f * 16 + 16 * ((N_FIRST + blk) // RING + 1))
                    pe.wait_ge(proj_act, f * 10 + (4 * J + max(m - 3, 0)))
                    if m < 2 * J:
                        ins = channels(s, m % J, bank[m % 4][:, 0:S])
                    else:
                        t = m - 2 * J
                        for c in range(C):
                            ins = M.matmul(bank[m % 4][:, :], hT[:, c, t * P:(t + 1) * P], slot3(s)[:, c, :],
                                           start=(c == 0), stop=(c == C - 1))
                    ins.then_inc(proj, 1)

                def score(h):
                    if h >= 2:
                        pe.wait_ge(neg_max, f * HALF_HEADS + (h - 1))
                    dst = bank[4 + h % 2]
                    M.matmul(dst[:, 0:P], qT[:, h, 0:P], kT[:, h, 0:P], start=True, stop=True)
                    M.matmul(dst[:, P:3 * P], qT[:, h, P:S], kT[:, h, :], start=True, stop=True).then_inc(scores, 1)

                pe.wait_ge(proj_act, f * 10 + (4 * J + 10))
                score(0)
                score(1)
                for h in range(HALF_HEADS):
                    g = f * HALF_HEADS
                    pe.wait_ge(probs_ready, g + (h + 1))
                    for i in range(3):
                        ins = M.transpose(bank[6][:, i * P:(i + 1) * P], probs[:, h % 2, i * P:(i + 1) * P], ident[:, :])
                    ins.then_inc(probs_turned, 1)
                    if h + 2 < HALF_HEADS:
                        score(h + 2)
                    pe.wait_ge(probsT_ready, g + (h + 1))
                    if h >= 1:
                        pe.wait_ge(att_copied, g + h)
                    hd = slice(h * P, (h + 1) * P)
                    M.matmul(bank[7][:, 0:P], v_tok[:, 0, hd], probsT[:, 0:P], start=True, stop=True)
                    M.matmul(bank[7][:, P:S], v_tok[:, 0, hd], probsT[:, P:2 * P], start=True, stop=False)
                    M.matmul(bank[7][:, P:S], v_tok[:, 1, hd], probsT[:, 2 * P:3 * P], start=False, stop=True).then_inc(att_out, 1)
                pe.wait_ge(att_copied, f * HALF_HEADS + HALF_HEADS)

            pe.wait_ge(ya_ready, J)
            pe.wait_ge(yc_ready, J)
            pe.wait_ge(proj_act, 4 * J + 10 * N_HALVES)
            for u in range(2 * (D // NB)):
                blk, t = OUT_BLOCK0 + u // 2, u % 2
                s = blk % RING
                if t == 0:
                    pe.wait_ge(w_loaded[s], 16 * (blk // RING + 1))
                if u >= 4:
                    pe.wait_ge(mixed_added, u - 3)
                for c in range(C):
                    ins = M.matmul(bank[u % 4][:, :], yT[:, c, t * P:(t + 1) * P], slot3(s)[:, c, :],
                                   start=(c == 0), stop=(c == C - 1))
                ins.then_inc(mixed, 1)

            pe.wait_ge(mixed_added, 2 * (D // NB))
            pe.wait_ge(h_ready, 2 * T)
            turn_all(C // 2)
            pe.wait_ge(turned_dve, C)
            pe.wait_ge(turned_act, C)
            W = GROUPS + E
            for t in range(T):
                for lo, n, w in ((0, GROUPS, rg), (GROUPS, E, re)):
                    dst = bank[4][:, t * W + lo:t * W + lo + n]
                    for c in range(C):
                        M.matmul(dst, hT[:, c, t * P:(t + 1) * P], w[:, c * n:(c + 1) * n], start=(c == 0), stop=False)
                    ins = M.matmul(dst, ones[0:1, :], rbias[:, lo:lo + n], start=False, stop=True)
            ins.then_inc(routed, 1)

            pe.wait_ge(chosen_ready, 1)
            pe.wait_ge(consts, CONSTS)
            for t in range(T):
                ins = M.matmul(bank[5][0:E, 0:P], chosen[:, 2, t, :], ones[:, :], start=(t == 0), stop=(t == T - 1))
            ins.then_inc(cnt_done, 1)
            pe.wait_ge(cnt_copied, 1)
            for t in range(T):
                dst = bank[4][:, 128 + t * E:128 + (t + 1) * E]
                M.matmul(dst, before[:, :], chosen[:, 2, t, :], start=True, stop=False)
                for tt in range(t):
                    M.matmul(dst, ones[:, :], chosen[:, 2, tt, :], start=False, stop=False)
                M.matmul(dst, cntT[:, :], before[0:E, 0:E], start=False, stop=True)
            M.matmul(bank[4][:, 192:192 + E], cntT[:, :], before[0:E, 0:E], start=True, stop=True)
            for t in range(T):
                ins = M.matmul(bank[4][:, 224:224 + E], ones[:, :], chosen[:, 2, t, :], start=(t == 0), stop=(t == T - 1))
            ins.then_inc(pos_done, 1)

            pe.wait_ge(pick_ready, T)
            for c in range(C):
                if c >= 4:
                    pe.wait_ge(sorted_act if c % 2 else sorted_dve, (c - 4) // 2 + 1)
                for t in range(T):
                    ins = M.matmul(bank[c % 4][:, :], h_tok_c[:, t, c, :], pick[:, t, :], start=(t == 0), stop=(t == T - 1))
                ins.then_inc(sorted_done, 1)
            pe.wait_ge(sorted_act, C // 2)
            pe.wait_ge(sorted_dve, C // 2)

            def expert_in(which, t, done):
                pe.wait_ge(w_loaded[which], t * 16 + 16 * (MOE_N + 1))
                for c in range(C):
                    ins = M.matmul(bank[which][:, :], x_win[:, c, :], slot3(which)[:, c, :], start=(c == 0), stop=(c == C - 1))
                ins.then_inc(done, 1)

            def turn_hidden(t):
                pe.wait_ge(hidden_ready, t + 1)
                for j in range(J):
                    ins = M.transpose(bank[2][:, j * P:(j + 1) * P],
                                      hidden.rearrange("p (k j) -> p j k", j=J)[:, j, :], ident[:, :])
                ins.then_inc(hidden_turned, 1)

            def down(t):
                pe.wait_ge(hiddenT_ready, t + 1)
                pe.wait_ge(w_loaded[2], t * 16 + 16 * (MOE_N + 1))
                w = ring[2][:, :].rearrange("p (j n) -> p j n", j=J)
                for b in range(D // NB):
                    if b == 0:
                        pe.wait_ge(y_act, 2 * t + 2)
                    if b == 2:
                        pe.wait_ge(y_dve, 2 * t + 2)
                    for j in range(J):
                        ins = M.matmul(bank[4 + b][:, :], hiddenT[:, j, :], w[:, j, b * NB:(b + 1) * NB],
                                       start=(j == 0), stop=(j == J - 1))
                    ins.then_inc(down_done, 1)

            pe.wait_ge(win_ready, 1)
            expert_in(0, 0, gate_done)
            expert_in(1, 0, up_done)
            with pe.Fori(1, E) as e:
                pe.wait_ge(win_ready, e + 1)
                pe.wait_ge(silu_done, e)
                expert_in(0, e, gate_done)
                turn_hidden(e - 1)
                expert_in(1, e, up_done)
                down(e - 1)
            turn_hidden(E - 1)
            down(E - 1)
            pe.wait_ge(tables_ready, 1)
            flag = pe.value_load(over_i[0:1, OVER:OVER + 1], min_val=0, max_val=E)
            with pe.If(flag > 0):
                with pe.Fori(E, E + OVER) as t:
                    pe.wait_ge(win_ready, t + 1)
                    expert_in(0, t, gate_done)
                    expert_in(1, t, up_done)
                    turn_hidden(t)
                    down(t)


_INS = ["x", "norm1_g", "w_in", "conv_a_w", "conv_c_w", "conv_c_b", "ln_c_g", "ln_c_b", "w_out", "norm2_g",
        "router_g_w", "router_g_b", "router_e_w", "router_e_b", "w_gate", "w_up", "w_down", "final_g"]


def kernel(**inputs):
    import numpy as np
    import concourse.bacc as bacc
    from concourse.bass_utils import run_bass_kernel_spmd

    nc = bacc.Bacc("TRN2", target_bir_lowering=False, num_devices=1)
    arrays, aps = {}, {}
    for name in _INS:
        arr = np.ascontiguousarray(inputs[name])
        arrays[f"in_{name}"] = arr
        aps[name] = nc.dram_tensor(f"in_{name}", arr.shape, mybir.dt.from_np(arr.dtype), kind="ExternalInput").ap()
    out = nc.dram_tensor("out", (1, S, D), F32, kind="ExternalOutput").ap()
    y_sorted = nc.dram_tensor("y_sorted", (SLOTS, D), F32, kind="Internal").ap()
    hybrid_moe_program(nc, aps, out[0], y_sorted)
    result = run_bass_kernel_spmd(nc, [arrays], core_ids=[0])
    return result.results[0]["out"]
```

```python
from contextlib import ExitStack

import concourse.bass as bass
from concourse import mybir

ALU = mybir.AluOpType
ACT = mybir.ActivationFunctionType
AX = mybir.AxisListType
F32 = mybir.dt.float32
F32R = mybir.dt.float32r
I32 = mybir.dt.int32
U32 = mybir.dt.uint32

P = 128
S = 256
T = S // P
D = 2048
C = D // P
NB = 512
J = NB // P
N_HEADS = 8
HALF_HEADS = 4
TAPS_A, TAPS_C = 3, 31
GROUPS, PER_GROUP = 4, 8
E = GROUPS * PER_GROUP
SLOTS = 2 * S
OVER = 3
ROWS_ACT, ROWS_DVE = 2, 2
FEW = 32
EPS = 1e-6
STAGES = 4
PARTS = 3
CW = C * NB // STAGES
MASKED = -3.0e33

COL_BG, COL_CG, COL_XV, COL_Q, COL_K, COL_V, COL_A, COL_GATE = 0, 512, 1024, 1536, 2560, 3584, 4608, 5120
FIRST_BLOCKS = [COL_A, COL_GATE, COL_CG, COL_XV, COL_BG]
N_FIRST = len(FIRST_BLOCKS)
N_HALVES = N_HEADS // HALF_HEADS
OUT_BLOCK0 = N_FIRST + 3 * N_HALVES
MOE_BLOCK0 = OUT_BLOCK0 + D // NB
OVER_BLOCK0 = MOE_BLOCK0 + 3 * E
assert MOE_BLOCK0 % 3 == 0 and PARTS == 3 and C % STAGES == 0

R_WA, R_WC = 0, TAPS_A
R_CB = R_WC + TAPS_C
R_LG, R_LB = R_CB + 1, R_CB + 2
N_PAR = R_LB + 1


def hybrid_moe_program(nc, a, out, y_sorted):
    with ExitStack() as ctx:
        def sb(name, shape, dt=F32):
            return ctx.enter_context(nc.sbuf_tensor(name, shape, dt))

        def sem(name):
            return ctx.enter_context(nc.semaphore(name))

        x_tok = sb("x_tok", [P, T, D])
        stage = [sb(f"stage{m}", [P, CW]) for m in range(STAGES)]
        w_hi = [sb(f"w_hi{i}", [P, CW], F32R) for i in range(PARTS)]
        w_lo = [sb(f"w_lo{i}", [P, CW], F32R) for i in range(PARTS)]
        h_hi = sb("h_hi", [P, C * S], F32R)
        h_lo = sb("h_lo", [P, C * S], F32R)
        ZC = S + TAPS_A - 1
        HCW = S + TAPS_C - 1
        Q0, K0, V0 = 0, HALF_HEADS * S, 2 * HALF_HEADS * S
        CV0 = V0 + T * NB
        HC0 = CV0 + J * S
        TMP0 = HC0 + J * HCW
        Z0 = TMP0 + J * S
        SOFT = 3 * P
        assert Z0 + J * ZC - TMP0 >= HALF_HEADS * SOFT
        zone_u = sb("zone_u", [P, max(Z0 + J * ZC, (C + 1) * SLOTS)])

        def u3(at, a_, b_, pat="p (a b) -> p a b"):
            return zone_u[:, at:at + a_ * b_].rearrange(pat, a=a_)

        hT_hi, hT_lo = (z[:, :].rearrange("p (c s) -> p c s", c=C) for z in (h_hi, h_lo))
        h_tok = u3(0, T, D)
        h_tok_c = zone_u[:, 0:T * D].rearrange("p (t k c) -> p t c k", t=T, c=C)
        h2T = u3(T * D, C, S)
        par = zone_u[0:N_PAR, T * D:T * D + NB]
        rg = zone_u[:, T * D + NB:T * D + NB + C * GROUPS]
        re = zone_u[:, T * D + 2 * NB:T * D + 2 * NB + C * E]
        qT, kT = u3(Q0, HALF_HEADS, S), u3(K0, HALF_HEADS, S)
        v_tok = u3(V0, T, NB)
        cvT, tmpT = u3(CV0, J, S), u3(TMP0, J, S)
        sqT = u3(TMP0, J, S)
        hcT, zT = u3(HC0, J, HCW), u3(Z0, J, ZC)
        logits = u3(TMP0, HALF_HEADS, SOFT)
        x_sorted = u3(0, C, SLOTS)
        x_sorted_pad = zone_u[:, C * SLOTS:C * SLOTS + P]
        win_hi, win_lo = (z[:, 0:C * P].rearrange("p (c n) -> p c n", c=C) for z in (h_hi, h_lo))
        hiddenT_hi, hiddenT_lo = (z[:, C * P:C * P + NB] for z in (h_hi, h_lo))
        pick = h_hi[:, C * P + NB:C * P + NB + T * SLOTS].rearrange("p (t n) -> p t n", t=T)

        ident = sb("ident", [P, P])
        warm = sb("warm", [1, 1])
        ones = sb("ones", [P, P])
        before = sb("before", [P, P])
        bias_d = sb("bias_d", [P, 3 * P])
        rstdT = sb("rstdT", [P, S])
        parT = sb("parT", [P, J, N_PAR])
        g1 = sb("g1", [P, C])
        g2 = sb("g2", [P, C])
        rw = sb("rw", [P, C, GROUPS + E])
        rbias = sb("rbias", [GROUPS + E, 1])
        small = sb("small", [P, 64])
        lg = sb("lg", [P, T, GROUPS + E])
        r4 = sb("r4", [P, 4, T, GROUPS])
        r8 = sb("r8", [P, 6, T, PER_GROUP])
        sq_parts = r8[:, 5, :, 0:D // NB]
        r32 = sb("r32", [P, 4, T, E])
        chosen = sb("chosen", [P, 3, T, E])
        logitsT = zone_u[0:GROUPS + E, C * SLOTS + 2 * P:C * SLOTS + 2 * P + S]
        cntT = zone_u[0:E, C * SLOTS + P:C * SLOTS + 2 * P]
        starts = sb("starts", [P, E + OVER + 1])
        counts = sb("counts", [P, E + OVER])
        over = sb("over", [P, 4, E])
        row_of = sb("row_of", [P, E + OVER])
        ramp = sb("ramp", [P, E])
        iota_row = sb("iota_row", [P, SLOTS])
        iota_p = sb("iota_p", [P, 1])
        start_i = sb("start_i", [1, E + OVER + 1], I32)
        count_i = sb("count_i", [1, E + OVER], I32)
        over_i = sb("over_i", [1, 2 * OVER], I32)
        row_i = sb("row_i", [P, E + OVER], I32)
        row_now = sb("row_now", [P, 1], I32)
        slot_i = sb("slot_i", [P, 2 * T], I32)

        with ExitStack() as mixers:
            y_hi, y_lo = (mixers.enter_context(nc.sbuf_tensor(n, [P, C * S], F32R)) for n in ("y_hi", "y_lo"))
        y_rows = sb("y_rows", [P, D])
        silu_g = sb("silu_g", [P, NB])
        hidden = sb("hidden", [P, NB])
        final_w = sb("final_w", [P, D])
        yT_hi, yT_lo = (z[:, :].rearrange("p (c s) -> p c s", c=C) for z in (y_hi, y_lo))
        h2_hi, h2_lo = (z[:, :].rearrange("p (t d) -> p t d", t=T) for z in (y_hi, y_lo))
        h2_hi_c, h2_lo_c = (z[:, :].rearrange("p (t k c) -> p t c k", t=T, c=C) for z in (y_hi, y_lo))

        bank = [ctx.enter_context(nc.psum_tensor(f"bank{i}", [P, NB], F32)) for i in range(8)]

        x_loaded = [sem(f"x_loaded{t}") for t in range(T)]
        par_loaded = sem("par_loaded")
        router_loaded = sem("router_loaded")
        w_loaded = [sem(f"w_loaded{m}") for m in range(STAGES)]
        hi_made = sem("hi_made")
        lo_made = sem("lo_made")
        used = sem("used")
        consts = sem("consts")
        pads = sem("pads")
        rw_ready = sem("rw_ready")
        lt_done = sem("lt_done")
        lt_copied = sem("lt_copied")
        starts_ready = sem("starts_ready")
        pool_step = sem("pool_step")
        par_turned = sem("par_turned")
        par_ready = sem("par_ready")
        sum_sq = sem("sum_sq")
        sq_made = sem("sq_made")
        warm_set = sem("warm_set")
        mean_sq = sem("mean_sq")
        root = sem("root")
        h_ready = sem("h_ready")
        turned = sem("turned")
        turned_h2 = sem("turned_h2")
        h2_lo_made = sem("h2_lo_made")
        short_tap = sem("short_tap")
        turned_dve = sem("turned_dve")
        turned_act = sem("turned_act")
        proj_act = sem("proj_act")
        proj_dve = sem("proj_dve")
        conv_in = sem("conv_in")
        dve_step = sem("dve_step")
        act_step = sem("act_step")
        conv_tap = sem("conv_tap")
        conv_done = sem("conv_done")
        ln_mean = sem("ln_mean")
        ln_scaled = sem("ln_scaled")
        y_hi_made = sem("y_hi_made")
        y_f32 = sem("y_f32")
        ln_out = sem("ln_out")
        h2_hi_made = sem("h2_hi_made")
        win_hi_made = sem("win_hi_made")
        hidden_hi = sem("hidden_hi")
        y_act = sem("y_act")
        ln_centred = sem("ln_centred")
        ln_square = sem("ln_square")
        ln_var = sem("ln_var")
        ln_eps = sem("ln_eps")
        ln_root = sem("ln_root")
        ya_ready = sem("ya_ready")
        yc_ready = sem("yc_ready")
        scores = sem("scores")
        att_step = sem("att_step")
        neg_max = sem("neg_max")
        exps = sem("exps")
        probs_ready = sem("probs_ready")
        probs_turned = sem("probs_turned")
        probsT_ready = sem("probsT_ready")
        att_out = sem("att_out")
        att_copied = sem("att_copied")
        mixed_added = sem("mixed_added")
        routed = sem("routed")
        rt = sem("rt")
        rt_in = sem("rt_in")
        chosen_ready = sem("chosen_ready")
        cnt_done = sem("cnt_done")
        cnt_copied = sem("cnt_copied")
        pos_done = sem("pos_done")
        pick_ready = sem("pick_ready")
        sorted_done = sem("sorted_done")
        sorted_dve = sem("sorted_dve")
        sorted_act = sem("sorted_act")
        tables_ready = sem("tables_ready")
        first_hi = sem("first_hi")
        first_ready = sem("first_ready")
        win_ready = sem("win_ready")
        silu_done = sem("silu_done")
        hidden_ready = sem("hidden_ready")
        hidden_turned = sem("hidden_turned")
        hiddenT_ready = sem("hiddenT_ready")
        y_dve = sem("y_dve")
        row_ready = sem("row_ready")
        y_stored = sem("y_stored")
        store_started = sem("store_started")
        rows_free = sem("rows_free")
        fg_loaded = sem("fg_loaded")
        slot_ready = sem("slot_ready")
        gathered = [[sem(f"gathered{k}_{t}") for t in range(T)] for k in range(2)]
        fin_ms = sem("fin_ms")
        fin_added = sem("fin_added")
        fin_root = sem("fin_root")
        fin_ready = sem("fin_ready")
        stored = sem("stored")

        def col(i, n=1):
            return small[:, i:i + n]

        SS, MS, RT_, RSTD = col(0, 2), col(2, 2), col(4, 2), col(6, 2)
        NMAX, ESUM, ERCP, MAX = (small[:, 8 * i:8 * i + 8] for i in range(1, 5))
        GM, GS, GR, PGRP, KM4 = (col(20 + 2 * i, 2) for i in range(5))
        EM, ES, ER, Q1, Q2, KM8 = (col(30 + 2 * i, 2) for i in range(6))
        GATE1, GATE2, TOP = col(42, 2), col(44, 2), col(46, 2)
        SLOT = small[:, 48:52]
        KOV, NONE = small[:, 52:55], small[:, 55:58]

        FINAL_HALVES = (slice(0, D // 2), slice(D // 2, D))
        FIRST_CONSTS, CONSTS = 2, 7

        w_in = a["w_in"][0].rearrange("(p c) n -> p c n", c=C)
        w_out = a["w_out"][0].rearrange("(c p) n -> p c n", p=P)
        CM = C // STAGES

        def chunk(n):
            return n + 1

        def columns(w, c0):
            return [w[:, m * CM:(m + 1) * CM, bass.ds(c0, NB)] for m in range(STAGES)]

        def expert(which, e):
            w = a[("w_gate", "w_up", "w_down")[which]][0][bass.ds(e, 1)].rearrange("e (p x) n -> p (e x n)", p=P)
            return [w[:, m * CW:(m + 1) * CW] for m in range(STAGES)]

        def load(sp, b, chunks):
            for m, src in enumerate(chunks):
                if not (isinstance(b, int) and b == 0):
                    sp.wait_ge(lo_made, chunk(4 * b + (m - 4)))
                dst = stage[m][:, :]
                if len(src.shape) == 3:
                    dst = dst.rearrange("p (c n) -> p c n", c=CM)
                sp.dma_start(dst, src).then_inc(w_loaded[m], 16)

        def split_hi(act, b, br, m):
            act.wait_ge(w_loaded[m], b * 16 + 16)
            if not (isinstance(b, int) and 4 * b + m < PARTS):
                act.wait_ge(used, chunk(4 * b + (m - PARTS)))
            nc.scalar.activation(w_hi[(br + m) % PARTS][:, :], stage[m][:, :], ACT.Copy).then_inc(hi_made, 1)

        def split_lo(dve, b, br, m):
            i = (br + m) % PARTS
            dve.wait_ge(hi_made, chunk(4 * b + m))
            nc.vector.tensor_tensor(w_lo[i][:, :], stage[m][:, :], w_hi[i][:, :].bitcast(F32),
                                    ALU.subtract).then_inc(lo_made, 1)

        def x_sorted_from(first):
            return zone_u[:, bass.ds(first, C * SLOTS)].rearrange("p (c n) -> p c n", c=C)[:, :, 0:P]

        def g_block(e):
            return e * 3 + (MOE_BLOCK0 - 1)

        def over_block(t):
            return t * 3 + (OVER_BLOCK0 - 3 * E)

        SCORE_BANK, TURN_BANK, OUT_BANK = (6, 7, 0, 1), (2, 3, 6, 7), (4, 5, 0, 1)

        block = ctx.enter_context(nc.Block())

        @block.sync
        def _(sp):
            for t in range(T):
                sp.dma_start(x_tok[:, t, :], a["x"][0, t * P:(t + 1) * P, :]).then_inc(x_loaded[t], 16)
            for row, src in ((R_WA, a["conv_a_w"][0]), (R_WC, a["conv_c_w"][0]), (R_CB, a["conv_c_b"]),
                             (R_LG, a["ln_c_g"]), (R_LB, a["ln_c_b"])):
                sp.dma_start(par[row:row + src.shape[0], :], src).then_inc(par_loaded, 16)
            sp.dma_start(g1[:, :], a["norm1_g"][0].rearrange("(p c) -> p c", c=C)).then_inc(par_loaded, 16)
            for n, c0 in enumerate(FIRST_BLOCKS):
                load(sp, n, columns(w_in, c0))
                if n == 0:
                    sp.dma_start(g2[:, :], a["norm2_g"][0].rearrange("(p c) -> p c", c=C)).then_inc(router_loaded, 16)
                    sp.dma_start(rg[:, :], a["router_g_w"][0].rearrange("(p c) g -> p (c g)", c=C)).then_inc(router_loaded, 16)
                    sp.dma_start(re[:, :], a["router_e_w"][0].rearrange("(p c) g -> p (c g)", c=C)).then_inc(router_loaded, 16)
                    sp.dma_start(rbias[0:GROUPS, :], a["router_g_b"].rearrange("o g -> g o")).then_inc(router_loaded, 16)
                    sp.dma_start(rbias[GROUPS:, :], a["router_e_b"].rearrange("o g -> g o")).then_inc(router_loaded, 16)
            with sp.Fori(0, N_HALVES) as f:
                for m, c0 in enumerate((COL_Q, COL_K, COL_V)):
                    load(sp, f * 3 + (N_FIRST + m), columns(w_in, f * NB + c0))
            for b in range(D // NB):
                load(sp, OUT_BLOCK0 + b, columns(w_out, b * NB))
            load(sp, MOE_BLOCK0, expert(0, 0))
            load(sp, MOE_BLOCK0 + 1, expert(1, 0))
            sp.wait_ge(sorted_done, C)
            sp.dma_start(final_w[:, :], a["final_g"].rearrange("(o d) -> o d", o=1).broadcast_to([P, D])).then_inc(fg_loaded, 16)
            with sp.Fori(1, E) as e:
                load(sp, g_block(e), expert(0, e))
                load(sp, g_block(e) + 1, expert(1, e))
                load(sp, g_block(e) + 2, expert(2, e - 1))
            load(sp, g_block(E), expert(2, E - 1))
            sp.wait_ge(tables_ready, 1)
            flag = sp.value_load(over_i[0:1, OVER:OVER + 1], min_val=0, max_val=E)
            with sp.If(flag > 0):
                with sp.Fori(E, E + OVER) as t:
                    e = sp.value_load(over_i[0:1, bass.ds(t - E, 1)], min_val=0, max_val=E - 1)
                    for which in range(3):
                        load(sp, over_block(t) + which, expert(which, e))
            for t in range(T):
                for i, half in enumerate(FINAL_HALVES):
                    sp.wait_ge(fin_ready, 2 * t + i + 1)
                    sp.dma_start(out[t * P:(t + 1) * P, half], x_tok[:, t, half]).then_inc(stored, 16)
            sp.wait_ge(stored, 16 * 2 * T)

        @block.gpsimd
        def _(pool):
            step = [0]

            def link(ins):
                step[0] += 1
                ins.then_inc(pool_step, 1)
                pool.wait_ge(pool_step, step[0])

            pool.sem_inc(rows_free, 1)

            pool.memset(warm[:, :], 1.0).then_inc(warm_set, 1)
            pool.memset(ones[:, :], 1.0).then_inc(consts, 1)
            link(pool.memset(ident[:, :], 0.0))
            pool.affine_select(out=ident[:, :], in_=ident[:, :], compare_op=ALU.not_equal, fill=1.0,
                               base=0, pattern=[[-1, P]], channel_multiplier=1).then_inc(consts, 1)
            pool.iota(bias_d[:, 0:P], pattern=[[1, P]], base=0, channel_multiplier=-1,
                      allow_small_or_imprecise_dtypes=True)
            link(pool.iota(bias_d[:, P:3 * P], pattern=[[1, 2 * P]], base=-P, channel_multiplier=-1,
                           allow_small_or_imprecise_dtypes=True))
            pool.affine_select(out=bias_d[:, 0:P], in_=bias_d[:, 0:P], compare_op=ALU.is_ge, fill=MASKED,
                               base=0, pattern=[[-1, P]], channel_multiplier=1).then_inc(consts, 1)
            pool.affine_select(out=bias_d[:, P:3 * P], in_=bias_d[:, P:3 * P], compare_op=ALU.is_ge, fill=MASKED,
                               base=P, pattern=[[-1, 2 * P]], channel_multiplier=1).then_inc(consts, 1)
            link(pool.memset(before[:, :], 1.0))
            pool.affine_select(out=before[:, :], in_=before[:, :], compare_op=ALU.is_ge, fill=0.0,
                               base=-1, pattern=[[1, P]], channel_multiplier=-1).then_inc(consts, 1)
            pool.iota(ramp[:, :], pattern=[[-1, E]], base=E, channel_multiplier=0,
                      allow_small_or_imprecise_dtypes=True).then_inc(consts, 1)
            pool.iota(iota_p[:, :], pattern=[[1, 1]], base=0, channel_multiplier=1,
                      allow_small_or_imprecise_dtypes=True).then_inc(consts, 1)
            pool.iota(iota_row[:, :], pattern=[[1, SLOTS]], base=0, channel_multiplier=0,
                      allow_small_or_imprecise_dtypes=True).then_inc(consts, 1)
            pool.wait_ge(router_loaded, 16 * 5)
            pool.tensor_copy(rw[:, :, 0:GROUPS], rg.rearrange("p (c g) -> p c g", c=C)).then_inc(rw_ready, 1)
            pool.tensor_copy(rw[:, :, GROUPS:], re.rearrange("p (c g) -> p c g", c=C)).then_inc(rw_ready, 1)
            pool.wait_ge(rw_ready, 2)
            pool.wait_ge(turned, C // 2)
            pool.memset(zT[:, :, 0:TAPS_A - 1], 0.0).then_inc(pads, 1)
            pool.memset(hcT[:, :, 0:TAPS_C - 1], 0.0).then_inc(pads, 1)

            def store_rows(t):
                pool.wait_ge(y_act, ROWS_ACT * t + 2 * ROWS_ACT)
                pool.wait_ge(y_dve, ROWS_DVE * t + 2 * ROWS_DVE)
                pool.wait_ge(row_ready, t + 1)
                pool.sem_inc(store_started, 1)
                count = pool.value_load(count_i[0:1, bass.ds(t, 1)], min_val=0, max_val=S)
                for rows, has_these in ((FEW, count <= FEW), (P, count > FEW)):
                    with pool.If(has_these):
                        pool.indirect_dma_start(
                            out=y_sorted, out_offset=bass.IndirectOffsetOnAxis(ap=row_now[0:rows, 0:1], axis=0),
                            in_=y_rows[0:rows, :], in_offset=None, bounds_check=SLOTS - 1,
                            oob_is_err=False).then_inc(y_stored, 16)
                pool.wait_ge(y_stored, 16 * t + 16)
                pool.sem_inc(rows_free, 1)

            pool.wait_ge(tables_ready, 1)
            with pool.Fori(0, E) as e:
                store_rows(e)
            flag = pool.value_load(over_i[0:1, OVER:OVER + 1], min_val=0, max_val=E)
            with pool.If(flag > 0):
                with pool.Fori(E, E + OVER) as t:
                    store_rows(t)
            for t in range(T):
                for k in range(2):
                    pool.indirect_dma_start(
                        out=stage[k * T + t][:, :], out_offset=None, in_=y_sorted,
                        in_offset=bass.IndirectOffsetOnAxis(ap=slot_i[:, k * T + t:k * T + t + 1], axis=0),
                        bounds_check=SLOTS - 1, oob_is_err=True).then_inc(gathered[k][t], 16)

        @block.scalar
        def _(act):
            step = [0]

            def link(ins):
                step[0] += 1
                ins.then_inc(act_step, 1)
                act.wait_ge(act_step, step[0])

            act.wait_ge(warm_set, 1)
            nc.scalar.activation(warm[:, :], warm[:, :], ACT.Sqrt).then_inc(warm_set, 1)
            act.wait_ge(warm_set, 2)
            for t in range(T):
                act.wait_ge(x_loaded[t], 16)
                nc.scalar.activation(h_tok[:, t, :], x_tok[:, t, :], ACT.Square, accum_out=SS[:, t:t + 1]).then_inc(sum_sq, 1)
            act.wait_ge(mean_sq, 1)
            nc.scalar.activation(RT_, MS, ACT.Sqrt).then_inc(root, 1)

            split_hi(act, 0, 0, 0)
            act.wait_ge(par_loaded, 16 * 6)
            for k in range(C // 2):
                act.wait_ge(turned, k + 1)
                for i in range(2):
                    ins = nc.scalar.activation(hT_hi[:, 2 * k + i, :], bank[4 + k % 4][:, i * S:(i + 1) * S], ACT.Copy,
                                               scale=g1[:, 2 * k + i:2 * k + i + 1])
                ins.then_inc(turned_act, 1)

            def split_block(b, br, between):
                if b > 0:
                    split_hi(act, b, br, 0)
                split_hi(act, b, br, 1)
                between()
                split_hi(act, b, br, 2)
                split_hi(act, b, br, 3)

            def nothing():
                pass

            def a_out():
                act.wait_ge(pads, 2)
                act.wait_ge(used, chunk(3))
                for j in range(J):
                    nc.scalar.activation(hcT[:, j, TAPS_C - 1:HCW], bank[j][:, 0:S], ACT.Copy).then_inc(proj_act, 1)

            def gate_out():
                act.wait_ge(used, chunk(7))
                for j in range(J):
                    nc.scalar.activation(tmpT[:, j, :], bank[4 + j][:, 0:S], ACT.Sigmoid).then_inc(proj_act, 1)

            def cg_out():
                act.wait_ge(used, chunk(11))
                for j in range(J):
                    nc.scalar.activation(zT[:, j, TAPS_A - 1:ZC], bank[j][:, 0:S], ACT.Copy).then_inc(proj_act, 1)

            for b, out_of_former in enumerate((nothing, a_out, gate_out, cg_out, nothing)):
                split_block(b, b % 3, out_of_former)

            for m in range(PARTS):
                split_hi(act, N_FIRST, N_FIRST % 3, m)
            for j in range(J):
                act.wait_ge(y_f32, j + 1)
                nc.scalar.activation(yT_hi[:, j, :], tmpT[:, j, :], ACT.Copy).then_inc(y_hi_made, 1)

            with act.Fori(0, N_HALVES) as f:
                b0, g = f * 3 + N_FIRST, f * HALF_HEADS
                kb, vb, nb = (N_FIRST + 1) % 3, (N_FIRST + 2) % 3, N_FIRST % 3
                split_hi(act, b0, nb, 3)
                split_hi(act, b0 + 1, kb, 0)
                split_hi(act, b0 + 1, kb, 1)
                act.wait_ge(used, chunk(4 * b0 + 3))
                for j in range(J):
                    nc.scalar.activation(qT[:, j, :], bank[4 + j][:, 0:S], ACT.Copy, scale=float(P) ** -0.5).then_inc(proj_act, 1)
                split_hi(act, b0 + 1, kb, 2)
                split_hi(act, b0 + 1, kb, 3)
                split_hi(act, b0 + 2, vb, 0)
                split_hi(act, b0 + 2, vb, 1)
                act.wait_ge(used, chunk(4 * b0 + 7))
                for j in range(J):
                    nc.scalar.activation(kT[:, j, :], bank[j][:, 0:S], ACT.Copy).then_inc(proj_act, 1)
                split_hi(act, b0 + 2, vb, 2)
                split_hi(act, b0 + 2, vb, 3)
                for h in range(HALF_HEADS):
                    act.wait_ge(neg_max, g + (h + 1))
                    for lo, hi, i in ((0, P, 2 * h), (P, 3 * P, 2 * h + 1)):
                        nc.scalar.activation(logits[:, h, lo:hi], logits[:, h, lo:hi], ACT.Exp, bias=NMAX[:, i:i + 1],
                                             accum_out=ESUM[:, i:i + 1]).then_inc(exps, 1)
                split_hi(act, b0 + 3, nb, 0)
                split_hi(act, b0 + 3, nb, 1)
                act.wait_ge(used, chunk(4 * b0 + 11))
                for t in range(T):
                    nc.scalar.activation(v_tok[:, t, :], bank[4 + t][:, :], ACT.Copy).then_inc(proj_act, 1)
                for h in range(HALF_HEADS):
                    act.wait_ge(probs_turned, g + (h + 1))
                    nc.scalar.activation(logits[:, h, :], bank[TURN_BANK[h]][:, 0:SOFT], ACT.Copy).then_inc(probsT_ready, 1)
                for h in range(HALF_HEADS):
                    act.wait_ge(att_out, g + (h + 1))
                    nc.scalar.activation(yT_hi[:, bass.ds(g + (J + h), 1), :].rearrange("p a s -> p (a s)"),
                                         bank[OUT_BANK[h]][:, 0:S], ACT.Copy).then_inc(y_hi_made, 1)
                split_hi(act, b0 + 3, nb, 2)

            for j in range(J):
                act.wait_ge(ln_centred, j + 1)
                nc.scalar.activation(sqT[:, j, :], cvT[:, j, :], ACT.Square).then_inc(ln_square, 1)
            split_hi(act, OUT_BLOCK0, OUT_BLOCK0 % 3, 3)
            act.wait_ge(ln_eps, 1)
            nc.scalar.activation(rstdT[:, :], rstdT[:, :], ACT.Sqrt).then_inc(ln_root, 1)
            for j in range(J):
                act.wait_ge(ln_scaled, j + 1)
                nc.scalar.activation(cvT[:, j, :], cvT[:, j, :], ACT.Silu, bias=parT[:, j, R_LB:R_LB + 1],
                                     scale=parT[:, j, R_LG:R_LG + 1]).then_inc(ln_out, 1)
            for j in range(J):
                act.wait_ge(ln_out, j + 1)
                nc.scalar.activation(yT_hi[:, 3 * J + j, :], cvT[:, j, :], ACT.Copy).then_inc(y_hi_made, 1)
            nc.scalar.activation(warm[:, :], warm[:, :], ACT.Sqrt)

            def squares(b):
                for t in range(T):
                    act.wait_ge(mixed_added, 2 * b + t + 1)
                    nc.scalar.activation(zone_u[:, (2 * b + t) * NB:(2 * b + t + 1) * NB], x_tok[:, t, b * NB:(b + 1) * NB],
                                         ACT.Square, accum_out=sq_parts[:, t, b:b + 1]).then_inc(sq_made, 1)

            for b in range(1, D // NB):
                split_block(OUT_BLOCK0 + b, (OUT_BLOCK0 + b) % 3, (lambda: squares(b - 2)) if b > 1 else nothing)
            for b in range(D // NB - 2, D // NB):
                squares(b)

            act.wait_ge(mean_sq, 2)
            nc.scalar.activation(RT_, MS, ACT.Sqrt).then_inc(root, 1)
            act.wait_ge(router_loaded, 16 * 5)
            for k in range(1, C // 2, 2):
                act.wait_ge(turned, C // 2 + k + 1)
                for i in range(2):
                    nc.scalar.activation(h2T[:, 2 * k + i, :], bank[k % 4][:, i * S:(i + 1) * S], ACT.Copy,
                                         scale=g2[:, 2 * k + i:2 * k + i + 1]).then_inc(turned_act, 1)
            for m in range(PARTS):
                split_hi(act, MOE_BLOCK0, MOE_BLOCK0 % 3, m)
            for t in range(T):
                act.wait_ge(h_ready, T + t + 1)
                act.wait_ge(used, chunk(4 * MOE_BLOCK0 - 1))
                nc.scalar.activation(h2_hi[:, t, :], h_tok[:, t, :], ACT.Copy).then_inc(h2_hi_made, 1)

            act.wait_ge(rt_in, 1)
            nc.scalar.activation(r4[:, 1], r4[:, 0], ACT.Exp).then_inc(rt, 1)
            act.wait_ge(rt_in, 2)
            nc.scalar.activation(r8[:, 1], r8[:, 0], ACT.Exp).then_inc(rt, 1)
            act.wait_ge(cnt_done, 1)
            nc.scalar.activation(cntT, bank[5][0:E, 0:P], ACT.Copy).then_inc(cnt_copied, 1)
            def first_window(m):
                act.wait_ge(sorted_act, (m + 1) * CM // 2)
                act.wait_ge(sorted_dve, (m + 1) * CM // 2)
                nc.scalar.activation(win_hi[:, m * CM:(m + 1) * CM, :], x_sorted[:, m * CM:(m + 1) * CM, 0:P],
                                     ACT.Copy).then_inc(first_hi, 1)

            for c in range(1, C, 2):
                act.wait_ge(sorted_done, c + 1)
                nc.scalar.activation(x_sorted[:, c, :], bank[c % 4][:, :], ACT.Copy,
                                     scale=g2[:, c:c + 1]).then_inc(sorted_act, 1)
                if c % CM == CM - 1 and c >= CM:
                    first_window(c // CM - 1)
            first_window(STAGES - 1)

            def window(t):
                first = act.value_load(start_i[0:1, bass.ds(t, 1)], min_val=0, max_val=SLOTS)
                nc.scalar.activation(win_hi, x_sorted_from(first), ACT.Copy).then_inc(win_hi_made, 1)

            def silu_of(t):
                nc.scalar.activation(silu_g[:, :], bank[0][:, :], ACT.Silu).then_inc(silu_done, 1)

            def turn_out(t):
                act.wait_ge(hidden_turned, t + 1)
                nc.scalar.activation(hiddenT_hi, bank[2][:, :], ACT.Copy).then_inc(hidden_hi, 1)

            def rows_out(t, down_block):
                act.wait_ge(used, chunk(4 * down_block + 3))
                act.wait_ge(rows_free, t + 1)
                for i in range(ROWS_ACT):
                    nc.scalar.activation(y_rows[:, i * NB:(i + 1) * NB], bank[4 + i][:, :], ACT.Copy).then_inc(y_act, 1)

            act.sem_inc(y_act, ROWS_ACT)
            act.wait_ge(starts_ready, 1)
            b = MOE_BLOCK0
            split_hi(act, b, b % 3, 3)
            for m in range(2):
                split_hi(act, b + 1, (b + 1) % 3, m)
            act.wait_ge(used, chunk(4 * b + 3))
            silu_of(0)
            for m in range(2, 4):
                split_hi(act, b + 1, (b + 1) % 3, m)

            def expert_round(e, former_rows):
                b, br = g_block(e), (MOE_BLOCK0 + 2) % 3
                split_hi(act, b, br, 0)
                split_hi(act, b, br, 1)
                if former_rows:
                    rows_out(e - 2, b - 1)
                else:
                    act.wait_ge(used, chunk(4 * (b - 1) + 3))
                    window(e)
                split_hi(act, b, br, 2)
                split_hi(act, b, br, 3)
                split_hi(act, b + 1, br + 1, 0)
                split_hi(act, b + 1, br + 1, 1)
                turn_out(e - 1)
                split_hi(act, b + 1, br + 1, 2)
                silu_of(e)
                split_hi(act, b + 1, br + 1, 3)
                split_hi(act, b + 2, br + 2, 0)
                split_hi(act, b + 2, br + 2, 1)
                split_hi(act, b + 2, br + 2, 2)
                split_hi(act, b + 2, br + 2, 3)
                window(e + 1)

            expert_round(1, False)
            with act.Fori(2, E) as e:
                expert_round(e, True)
            for m in range(2):
                split_hi(act, g_block(E), g_block(E) % 3, m)
            rows_out(E - 2, g_block(E) - 1)
            turn_out(E - 1)
            for m in range(2, 4):
                split_hi(act, g_block(E), g_block(E) % 3, m)
            rows_out(E - 1, g_block(E))
            nc.scalar.activation(warm[:, :], warm[:, :], ACT.Sqrt)
            act.wait_ge(tables_ready, 1)
            flag = act.value_load(over_i[0:1, OVER:OVER + 1], min_val=0, max_val=E)
            with act.If(flag > 0):
                with act.Fori(E, E + OVER) as t:
                    b, br = over_block(t), OVER_BLOCK0 % 3
                    for m in range(4):
                        split_hi(act, b, br, m)
                    for m in range(3):
                        split_hi(act, b + 1, br + 1, m)
                    silu_of(t)
                    split_hi(act, b + 1, br + 1, 3)
                    split_hi(act, b + 2, br + 2, 0)
                    split_hi(act, b + 2, br + 2, 1)
                    turn_out(t)
                    split_hi(act, b + 2, br + 2, 2)
                    window(t + 1)
                    split_hi(act, b + 2, br + 2, 3)
                    rows_out(t, b + 2)
            for t in range(T):
                act.wait_ge(fin_added, t + 1)
                nc.scalar.activation(zone_u[:, t * D:(t + 1) * D], x_tok[:, t, :], ACT.Square,
                                     accum_out=SS[:, t:t + 1]).then_inc(fin_root, 1)
                act.wait_ge(fin_ms, t + 1)
                nc.scalar.activation(RT_[:, t:t + 1], MS[:, t:t + 1], ACT.Sqrt).then_inc(fin_root, 1)

        @block.vector
        def _(dve):
            step = [0]

            def link(ins):
                step[0] += 1
                ins.then_inc(dve_step, 1)
                dve.wait_ge(dve_step, step[0])

            V = nc.vector

            def rstd_of(n):
                dve.wait_ge(sum_sq, 2 * n)
                V.tensor_scalar(MS, SS, 1.0 / D, EPS, ALU.mult, ALU.add).then_inc(mean_sq, 1)
                dve.wait_ge(root, n)
                link(V.reciprocal(RSTD, RT_))

            dve.sem_inc(att_copied, HALF_HEADS)

            rstd_of(1)
            for t in range(T):
                V.tensor_scalar(h_tok[:, t, :], x_tok[:, t, :], RSTD[:, t:t + 1], None, ALU.mult).then_inc(h_ready, 1)
            dve.wait_ge(par_turned, 1)
            V.tensor_copy(parT[:, :, :], bank[7][:, 0:J * N_PAR].rearrange("p (j n) -> p j n", j=J)).then_inc(par_ready, 1)
            split_lo(dve, 0, 0, 0)
            dve.wait_ge(par_loaded, 16 * 6)
            for k in range(C // 2):
                dve.wait_ge(turned_act, k + 1)
                for i in range(2):
                    c = 2 * k + i
                    ins = V.scalar_tensor_tensor(hT_lo[:, c, :], bank[4 + k % 4][:, i * S:(i + 1) * S], g1[:, c:c + 1],
                                                 hT_hi[:, c, :].bitcast(F32), ALU.mult, ALU.subtract)
                ins.then_inc(turned_dve, 1)

            def split_block(b, br, between=None):
                for m in range(1 if isinstance(b, int) and b == 0 else 0, 4):
                    split_lo(dve, b, br, m)
                    if between is not None:
                        between(m)

            def gated(m):
                if m != 2:
                    return
                for j in range(J):
                    dve.wait_ge(proj_act, J + j + 1)
                    row = hcT[:, j, TAPS_C - 1:HCW]
                    V.tensor_tensor(row, row, tmpT[:, j, :], ALU.mult).then_inc(conv_in, 1)
                dve.wait_ge(conv_in, J)
                for j in range(J):
                    V.tensor_scalar(cvT[:, j, :], hcT[:, j, 0:S], parT[:, j, R_WC:R_WC + 1],
                                    parT[:, j, R_CB:R_CB + 1], ALU.mult, ALU.add).then_inc(conv_tap, 1)

            def taps(first, last):
                with dve.Fori(first, last) as i:
                    for j in range(J):
                        dve.wait_ge(conv_tap, i * J + (j + 1 - J))
                        V.scalar_tensor_tensor(cvT[:, j, :], hcT[:, j, bass.ds(i, S)], parT[:, j, bass.ds(i + R_WC, 1)],
                                               cvT[:, j, :], ALU.mult, ALU.add).then_inc(conv_tap, 1)

            split_block(0, 0)
            dve.wait_ge(par_ready, 1)
            split_block(1, 1)
            split_block(2, 2, gated)
            split_block(3, 0, lambda m: taps(1 + m, 2 + m))

            def xv_out(m):
                if m == 1:
                    dve.wait_ge(used, chunk(4 * 3 + 3))
                    for j in range(J):
                        row = zT[:, j, TAPS_A - 1:ZC]
                        V.tensor_tensor(row, row, bank[4 + j][:, 0:S], ALU.mult).then_inc(proj_dve, 1)
                    dve.wait_ge(proj_dve, J)
                    for i in range(TAPS_A):
                        for j in range(J):
                            w = parT[:, j, R_WA + i:R_WA + i + 1]
                            if i == 0:
                                ins = V.tensor_scalar(tmpT[:, j, :], zT[:, j, 0:S], w, None, ALU.mult)
                            else:
                                dve.wait_ge(short_tap, (i - 1) * J + j + 1)
                                ins = V.scalar_tensor_tensor(tmpT[:, j, :], zT[:, j, i:i + S], w, tmpT[:, j, :],
                                                             ALU.mult, ALU.add)
                            ins.then_inc(short_tap, 1)

            split_block(4, 1, xv_out)
            for m in range(PARTS):
                split_lo(dve, N_FIRST, N_FIRST % 3, m)
            dve.wait_ge(short_tap, TAPS_A * J)
            dve.wait_ge(used, chunk(4 * 4 + 3))
            for j in range(J):
                V.tensor_tensor(tmpT[:, j, :], bank[j][:, 0:S], tmpT[:, j, :], ALU.mult).then_inc(y_f32, 1)
            for j in range(J):
                dve.wait_ge(y_hi_made, j + 1)
                V.tensor_tensor(yT_lo[:, j, :], tmpT[:, j, :], yT_hi[:, j, :].bitcast(F32), ALU.subtract).then_inc(ya_ready, 1)

            dve.wait_ge(consts, CONSTS)
            BETWEEN = (2, 2, 2, 2, 2, 1, 1, 1)
            PER_HALF = sum(BETWEEN)
            assert 1 + STAGES + N_HALVES * PER_HALF == TAPS_C
            with dve.Fori(0, N_HALVES) as f:
                A_STEPS = 3 * HALF_HEADS + 1
                b0, g = f * 3 + N_FIRST, f * HALF_HEADS
                kb, vb, nb = (N_FIRST + 1) % 3, (N_FIRST + 2) % 3, N_FIRST % 3
                done = 1 + STAGES
                for i, n in enumerate(BETWEEN):
                    if i >= 3:
                        split_lo(dve, b0 + (0 if i == 3 else 1), nb if i == 3 else kb, 3 if i == 3 else i - 4)
                    taps(f * PER_HALF + done, f * PER_HALF + (done + n))
                    done += n

                def att(ins, k):
                    ins.then_inc(att_step, 1)
                    dve.wait_ge(att_step, f * A_STEPS + k)

                def biased(h):
                    dve.wait_ge(scores, g + (h + 1))
                    att(V.scalar_tensor_tensor(logits[:, h, :], bias_d[:, :], 0.5 ** (h + 1),
                                               bank[SCORE_BANK[h]][:, 0:SOFT], ALU.mult, ALU.add), 2 * h + 1)
                    V.tensor_reduce(MAX[:, 2 * h:2 * h + 1], logits[:, h, 0:P], AX.X, ALU.max)
                    att(V.tensor_reduce(MAX[:, 2 * h + 1:2 * h + 2], logits[:, h, P:SOFT], AX.X, ALU.max), 2 * h + 2)
                    V.tensor_scalar(NMAX[:, 2 * h:2 * h + 2], MAX[:, 2 * h:2 * h + 2], -1.0, None, ALU.mult).then_inc(neg_max, 1)

                def normalised(h):
                    dve.wait_ge(exps, f * (2 * HALF_HEADS) + (2 * h + 2))
                    att(V.reciprocal(ERCP[:, 2 * h:2 * h + 2], ESUM[:, 2 * h:2 * h + 2]), 2 * HALF_HEADS + h + 1)
                    V.tensor_scalar(logits[:, h, 0:P], logits[:, h, 0:P], ERCP[:, 2 * h:2 * h + 1], None, ALU.mult)
                    V.tensor_scalar(logits[:, h, P:SOFT], logits[:, h, P:SOFT], ERCP[:, 2 * h + 1:2 * h + 2], None,
                                    ALU.mult).then_inc(probs_ready, 1)

                split_lo(dve, b0 + 2, vb, 0)
                split_lo(dve, b0 + 2, vb, 1)
                biased(0)
                biased(1)
                split_lo(dve, b0 + 2, vb, 2)
                biased(2)
                biased(3)
                split_lo(dve, b0 + 2, vb, 3)
                for h in range(HALF_HEADS):
                    normalised(h)
                att(V.tensor_scalar(bias_d[:, :], bias_d[:, :], 0.5 ** HALF_HEADS, None, ALU.mult), A_STEPS)
                split_lo(dve, b0 + 3, nb, 0)
                split_lo(dve, b0 + 3, nb, 1)
                for h in range(HALF_HEADS):
                    dve.wait_ge(y_hi_made, g + (J + h + 1))
                    at = bass.ds(g + (J + h), 1)
                    V.tensor_tensor(yT_lo[:, at, :].rearrange("p a s -> p (a s)"), bank[OUT_BANK[h]][:, 0:S],
                                    yT_hi[:, at, :].bitcast(F32).rearrange("p a s -> p (a s)"),
                                    ALU.subtract).then_inc(att_copied, 1)
                split_lo(dve, b0 + 3, nb, 2)

            dve.wait_ge(conv_tap, TAPS_C * J)
            V.engine_nop().then_inc(conv_done, 1)
            dve.wait_ge(ln_mean, 1)
            for j in range(J):
                V.scalar_tensor_tensor(cvT[:, j, :], bank[4][:, 0:S], -1.0 / NB, cvT[:, j, :], ALU.mult,
                                       ALU.add).then_inc(ln_centred, 1)
            split_lo(dve, OUT_BLOCK0, OUT_BLOCK0 % 3, 3)
            dve.wait_ge(ln_var, 1)
            V.tensor_scalar(rstdT[:, :], bank[5][:, 0:S], 1.0 / NB, EPS, ALU.mult, ALU.add).then_inc(ln_eps, 1)
            dve.wait_ge(ln_root, 1)
            link(V.reciprocal(rstdT[:, :], rstdT[:, :]))
            for j in range(J):
                V.tensor_tensor(cvT[:, j, :], cvT[:, j, :], rstdT[:, :], ALU.mult).then_inc(ln_scaled, 1)
            for j in range(J):
                dve.wait_ge(y_hi_made, J + N_HEADS + j + 1)
                V.tensor_tensor(yT_lo[:, 3 * J + j, :], cvT[:, j, :], yT_hi[:, 3 * J + j, :].bitcast(F32),
                                ALU.subtract).then_inc(yc_ready, 1)

            def add_mixed(b):
                dve.wait_ge(used, chunk(4 * (OUT_BLOCK0 + b) + 3))
                for t in range(T):
                    at = x_tok[:, t, b * NB:(b + 1) * NB]
                    V.tensor_tensor(at, at, bank[2 * b + t][:, :], ALU.add).then_inc(mixed_added, 1)

            for b in range(1, D // NB):
                split_block(OUT_BLOCK0 + b, (OUT_BLOCK0 + b) % 3, lambda m: add_mixed(b - 1) if m == 1 else None)
            add_mixed(D // NB - 1)
            dve.wait_ge(sq_made, 2 * (D // NB))
            V.tensor_reduce(SS, sq_parts, AX.X, ALU.add).then_inc(sum_sq, T)
            rstd_of(2)
            for t in range(T):
                V.tensor_scalar(h_tok[:, t, :], x_tok[:, t, :], RSTD[:, t:t + 1], None, ALU.mult).then_inc(h_ready, 1)
            dve.wait_ge(router_loaded, 16 * 5)
            for k in range(0, C // 2, 2):
                dve.wait_ge(turned, C // 2 + k + 1)
                for i in range(2):
                    V.tensor_scalar(h2T[:, 2 * k + i, :], bank[k % 4][:, i * S:(i + 1) * S],
                                    g2[:, 2 * k + i:2 * k + i + 1], None, ALU.mult).then_inc(turned_h2, 1)

            for m in range(PARTS):
                split_lo(dve, MOE_BLOCK0, MOE_BLOCK0 % 3, m)

            dve.wait_ge(lt_done, 1)
            V.tensor_scalar(logitsT, bank[5][0:GROUPS + E, 0:S], rbias[:, 0:1], None, ALU.add).then_inc(lt_copied, 1)
            dve.wait_ge(routed, 1)
            link(V.tensor_copy(lg[:, :, :], bank[4][:, 0:T * (GROUPS + E)].rearrange("p (t n) -> p t n", t=T)))
            lgrp = lg[:, :, 0:GROUPS]

            def spread(v, n):
                return v.unsqueeze(2).broadcast_to([P, T, n])

            link(V.tensor_reduce(GM, lgrp, AX.X, ALU.max))
            V.tensor_tensor(r4[:, 0], lgrp, spread(GM, GROUPS), ALU.subtract).then_inc(rt_in, 1)
            dve.wait_ge(rt, 1)
            link(V.tensor_reduce(GS, r4[:, 1], AX.X, ALU.add))
            link(V.reciprocal(GR, GS))
            link(V.tensor_tensor(r4[:, 1], r4[:, 1], spread(GR, GROUPS), ALU.mult))
            link(V.tensor_reduce(PGRP, r4[:, 1], AX.X, ALU.max))

            def first_max(dst, vals, top, key, km, n):
                link(V.tensor_tensor(key, vals, spread(top, n), ALU.is_equal))
                link(V.tensor_tensor(key, key, ramp[:, E - n:E].unsqueeze(1).broadcast_to([P, T, n]), ALU.mult))
                link(V.tensor_reduce(km, key, AX.X, ALU.max))
                link(V.tensor_tensor(dst, key, spread(km, n), ALU.is_equal))

            first_max(r4[:, 3], r4[:, 1], PGRP, r4[:, 2], KM4, GROUPS)
            for t in range(T):
                link(V.tensor_tensor(r32[:, 0, t, :].rearrange("p (g e) -> p g e", g=GROUPS),
                                     lg[:, t, GROUPS:].rearrange("p (g e) -> p g e", g=GROUPS),
                                     r4[:, 3, t, :].unsqueeze(2).broadcast_to([P, GROUPS, PER_GROUP]), ALU.mult))
                link(V.tensor_reduce(r8[:, 2, t, :], r32[:, 0, t, :].rearrange("p (g e) -> p e g", g=GROUPS), AX.X, ALU.add))
            link(V.tensor_reduce(EM, r8[:, 2], AX.X, ALU.max))
            V.tensor_tensor(r8[:, 0], r8[:, 2], spread(EM, PER_GROUP), ALU.subtract).then_inc(rt_in, 1)
            dve.wait_ge(rt, 2)
            link(V.tensor_reduce(ES, r8[:, 1], AX.X, ALU.add))
            link(V.reciprocal(ER, ES))
            link(V.tensor_tensor(r8[:, 1], r8[:, 1], spread(ER, PER_GROUP), ALU.mult))
            link(V.tensor_reduce(Q1, r8[:, 1], AX.X, ALU.max))
            first_max(r8[:, 3], r8[:, 1], Q1, r8[:, 2], KM8, PER_GROUP)
            link(V.scalar_tensor_tensor(r8[:, 1], r8[:, 3], -2.0, r8[:, 1], ALU.mult, ALU.add))
            link(V.tensor_reduce(Q2, r8[:, 1], AX.X, ALU.max))
            first_max(r8[:, 4], r8[:, 1], Q2, r8[:, 2], KM8, PER_GROUP)
            link(V.tensor_tensor(TOP, Q1, Q2, ALU.add))
            link(V.reciprocal(TOP, TOP))
            link(V.tensor_tensor(GATE1, PGRP, Q1, ALU.mult))
            link(V.tensor_tensor(GATE1, GATE1, TOP, ALU.mult))
            link(V.tensor_tensor(GATE2, PGRP, Q2, ALU.mult))
            link(V.tensor_tensor(GATE2, GATE2, TOP, ALU.mult))
            for k in range(2):
                for t in range(T):
                    link(V.tensor_tensor(chosen[:, k, t, :].rearrange("p (g e) -> p g e", g=GROUPS),
                                         r4[:, 3, t, :].unsqueeze(2).broadcast_to([P, GROUPS, PER_GROUP]),
                                         r8[:, 3 + k, t, :].unsqueeze(1).broadcast_to([P, GROUPS, PER_GROUP]), ALU.mult))
            V.tensor_tensor(chosen[:, 2], chosen[:, 0], chosen[:, 1], ALU.add).then_inc(chosen_ready, 1)

            for t in range(T):
                dve.wait_ge(h2_hi_made, t + 1)
                V.tensor_tensor(h2_lo[:, t, :], h_tok[:, t, :], h2_hi[:, t, :].bitcast(F32),
                                ALU.subtract).then_inc(h2_lo_made, 1)

            dve.wait_ge(pos_done, 1)
            posv = bank[4][:, 128:128 + T * E].rearrange("p (t e) -> p t e", t=T)
            for k in range(2):
                link(V.tensor_tensor(r32[:, k], chosen[:, k], posv, ALU.mult))
                link(V.tensor_reduce(SLOT[:, k * T:(k + 1) * T], r32[:, k], AX.X, ALU.add))
            dve.wait_ge(consts, CONSTS + 1)
            for t in range(T):
                link(V.tensor_scalar(pick[:, t, :], iota_row[:, :], SLOT[:, t:t + 1], None, ALU.is_equal))
                V.scalar_tensor_tensor(pick[:, t, :], iota_row[:, :], SLOT[:, T + t:T + t + 1], pick[:, t, :].bitcast(F32), ALU.is_equal,
                                       ALU.add).then_inc(pick_ready, 1)
            link(V.tensor_copy(slot_i[:, :], SLOT))
            link(V.memset(starts[:, E + OVER:], 0.0))
            link(V.tensor_copy(starts[:, 0:E], bank[4][:, 192:192 + E]))
            link(V.tensor_copy(counts[:, 0:E], bank[4][:, 224:224 + E]))
            V.memset(x_sorted_pad, 0.0)
            V.tensor_copy(start_i[:, 0:E], starts[0:1, 0:E]).then_inc(starts_ready, 1)

            def first_window(m):
                dve.wait_ge(first_hi, m + 1)
                at = slice(m * CM, (m + 1) * CM)
                V.tensor_tensor(win_lo[:, at, :], x_sorted[:, at, 0:P], win_hi[:, at, :].bitcast(F32),
                                ALU.subtract).then_inc(first_ready, 1)

            for c in range(0, C, 2):
                dve.wait_ge(sorted_done, c + 1)
                V.tensor_scalar(x_sorted[:, c, :], bank[c % 4][:, :], g2[:, c:c + 1], None, ALU.mult).then_inc(sorted_dve, 1)
                if c % CM == CM - 2 and c >= 2 * CM:
                    first_window(c // CM - 2)
            for m in range(STAGES - 2, STAGES):
                first_window(m)

            def window(t):
                first = dve.value_load(start_i[0:1, bass.ds(t, 1)], min_val=0, max_val=SLOTS)
                dve.wait_ge(win_hi_made, t)
                V.tensor_tensor(win_lo, x_sorted_from(first), win_hi.bitcast(F32), ALU.subtract).then_inc(win_ready, 1)

            def hidden_of(t):
                dve.wait_ge(silu_done, t + 1)
                V.tensor_tensor(hidden[:, :], silu_g[:, :], bank[1][:, :], ALU.mult).then_inc(hidden_ready, 1)

            def turn_out(t):
                dve.wait_ge(hidden_hi, t + 1)
                V.tensor_tensor(hiddenT_lo, bank[2][:, :], hiddenT_hi.bitcast(F32), ALU.subtract).then_inc(hiddenT_ready, 1)

            def rows_out(t, down_block):
                dve.wait_ge(used, chunk(4 * down_block + 3))
                dve.wait_ge(rows_free, t + 1)
                V.tensor_copy(row_now[:, :], row_i[:, bass.ds(t, 1)]).then_inc(row_ready, 1)
                for i in range(ROWS_ACT, D // NB):
                    V.tensor_copy(y_rows[:, i * NB:(i + 1) * NB], bank[4 + i][:, :]).then_inc(y_dve, 1)

            def begin_tables():
                link(V.tensor_scalar(over[:, 0, :], counts[:, 0:E], float(P), None, ALU.is_gt))
                link(V.tensor_tensor(over[:, 0, :], over[:, 0, :], ramp[:, :], ALU.mult))
                link(V.tensor_scalar(over[:, 3, :], starts[:, 0:E], float(P), None, ALU.add))
                take_crowded(range(OVER - 1))

            def take_crowded(which):
                for i in which:
                    link(V.tensor_reduce(KOV[:, i:i + 1], over[:, 0, :], AX.X, ALU.max))
                    link(V.tensor_scalar(over[:, 1, :], ramp[:, :], KOV[:, i:i + 1], None, ALU.is_equal))
                    link(V.tensor_tensor(over[:, 2, :], over[:, 1, :], over[:, 3, :], ALU.mult))
                    link(V.tensor_reduce(starts[:, E + i:E + i + 1], over[:, 2, :], AX.X, ALU.add))
                    link(V.tensor_tensor(over[:, 2, :], over[:, 1, :], counts[:, 0:E], ALU.mult))
                    link(V.tensor_reduce(counts[:, E + i:E + i + 1], over[:, 2, :], AX.X, ALU.add))
                    link(V.scalar_tensor_tensor(over[:, 0, :], over[:, 0, :], KOV[:, i:i + 1], over[:, 0, :],
                                                ALU.is_lt, ALU.mult))

            def finish_tables():
                take_crowded(range(OVER - 1, OVER))
                link(V.tensor_scalar(counts[:, E:], counts[:, E:], -float(P), None, ALU.add))
                link(V.tensor_scalar(row_of[:, :], counts[:, :], iota_p[:, 0:1], float(4 * SLOTS), ALU.is_le, ALU.mult))
                link(V.tensor_tensor(row_of[:, :], row_of[:, :], starts[:, 0:E + OVER], ALU.add))
                link(V.tensor_scalar(row_of[:, :], row_of[:, :], iota_p[:, 0:1], None, ALU.add))
                link(V.tensor_copy(row_i[:, :], row_of[:, :]))
                link(V.tensor_scalar(count_i[:, :], counts[0:1, :], 0.0, None, ALU.max))
                V.tensor_copy(start_i[:, E:], starts[0:1, E:])
                link(V.tensor_scalar(NONE, KOV, -1.0, float(E), ALU.mult, ALU.add))
                link(V.tensor_scalar(NONE, NONE, float(E - 1), None, ALU.min))
                link(V.tensor_copy(over_i[:, 0:OVER], NONE[0:1, :]))
                link(V.tensor_copy(over_i[:, OVER:2 * OVER], KOV[0:1, :]))
                V.engine_nop().then_inc(tables_ready, 1)

            dve.sem_inc(y_dve, ROWS_DVE)
            b = MOE_BLOCK0
            split_lo(dve, b, b % 3, 3)
            split_block(b + 1, (b + 1) % 3)
            begin_tables()

            def expert_round(e, former_rows):
                b, br = g_block(e), (MOE_BLOCK0 + 2) % 3
                split_lo(dve, b, br, 0)
                if former_rows:
                    hidden_of(e - 1)
                split_lo(dve, b, br, 1)
                if former_rows:
                    rows_out(e - 2, b - 1)
                else:
                    dve.wait_ge(used, chunk(4 * (b - 1) + 3))
                    window(e)
                    hidden_of(e - 1)
                split_lo(dve, b, br, 2)
                if not former_rows:
                    finish_tables()
                split_lo(dve, b, br, 3)
                split_lo(dve, b + 1, br + 1, 0)
                split_lo(dve, b + 1, br + 1, 1)
                turn_out(e - 1)
                split_lo(dve, b + 1, br + 1, 2)
                split_lo(dve, b + 1, br + 1, 3)
                for m in range(4):
                    split_lo(dve, b + 2, br + 2, m)
                window(e + 1)

            expert_round(1, False)
            with dve.Fori(2, E) as e:
                expert_round(e, True)
            split_lo(dve, g_block(E), g_block(E) % 3, 0)
            hidden_of(E - 1)
            rows_out(E - 2, g_block(E) - 1)
            turn_out(E - 1)
            for m in range(1, 4):
                split_lo(dve, g_block(E), g_block(E) % 3, m)
            rows_out(E - 1, g_block(E))
            flag = dve.value_load(over_i[0:1, OVER:OVER + 1], min_val=0, max_val=E)
            with dve.If(flag > 0):
                with dve.Fori(E, E + OVER) as t:
                    b, br = over_block(t), OVER_BLOCK0 % 3
                    split_block(b, br)
                    split_block(b + 1, br + 1)
                    dve.wait_ge(used, chunk(4 * b + 7))
                    hidden_of(t)
                    split_lo(dve, b + 2, br + 2, 0)
                    split_lo(dve, b + 2, br + 2, 1)
                    turn_out(t)
                    split_lo(dve, b + 2, br + 2, 2)
                    window(t + 1)
                    split_lo(dve, b + 2, br + 2, 3)
                    rows_out(t, b + 2)

            for t in range(T):
                dve.wait_ge(gathered[0][t], 16)
                link(V.scalar_tensor_tensor(x_tok[:, t, :], stage[t][:, :], GATE1[:, t:t + 1],
                                            x_tok[:, t, :], ALU.mult, ALU.add))
                dve.wait_ge(gathered[1][t], 16)
                V.scalar_tensor_tensor(x_tok[:, t, :], stage[T + t][:, :], GATE2[:, t:t + 1],
                                       x_tok[:, t, :], ALU.mult, ALU.add).then_inc(fin_added, 1)
            dve.wait_ge(fg_loaded, 16)
            for t in range(T):
                dve.wait_ge(fin_root, 2 * t + 1)
                V.tensor_scalar(MS[:, t:t + 1], SS[:, t:t + 1], 1.0 / D, EPS, ALU.mult, ALU.add).then_inc(fin_ms, 1)
                dve.wait_ge(fin_root, 2 * t + 2)
                link(V.reciprocal(RSTD[:, t:t + 1], RT_[:, t:t + 1]))
                for half in FINAL_HALVES:
                    V.scalar_tensor_tensor(x_tok[:, t, half], x_tok[:, t, half], RSTD[:, t:t + 1], final_w[:, half],
                                           ALU.mult, ALU.mult).then_inc(fin_ready, 1)

        @block.tensor
        def _(pe):
            M = nc.tensor

            def turn_all(first_bank, even):
                for k in range(C // 2):
                    if even is None and k == 3:
                        pe.wait_ge(par_ready, 1)
                    if k >= 4:
                        if even is None:
                            pe.wait_ge(turned_dve, k - 3)
                        elif k % 2:
                            pe.wait_ge(turned_act, C // 2 + k - 3)
                        else:
                            pe.wait_ge(even, k - 2)
                    for i in range(2):
                        for t in range(T):
                            ins = M.transpose(bank[first_bank + k % 4][:, i * S + t * P:i * S + (t + 1) * P],
                                              h_tok_c[:, t, 2 * k + i, :], ident[:, :])
                    ins.then_inc(turned, 1)

            pe.wait_ge(consts, FIRST_CONSTS)
            pe.wait_ge(par_loaded, 16 * 6)
            for j in range(J):
                ins = M.transpose(bank[7][:, j * N_PAR:(j + 1) * N_PAR], par[:, j * P:(j + 1) * P], ident[0:N_PAR, 0:N_PAR])
            ins.then_inc(par_turned, 1)
            pe.wait_ge(h_ready, T)
            turn_all(4, None)

            def parts(b, br, m):
                pe.wait_ge(lo_made, chunk(4 * b + m))
                i = (br + m) % PARTS
                return w_hi[i][:, :], w_lo[i][:, :]

            def products(dst, pairs, start, stop):
                for i, (stationary, moving) in enumerate(pairs):
                    ins = M.matmul(dst, stationary, moving, start=start and i == 0, stop=stop and i == 2)
                return ins

            def channels(b, br, banks, before_chunk=None):
                for m in range(STAGES):
                    if before_chunk is not None:
                        before_chunk(m)
                    hi, lo = parts(b, br, m)
                    for j in range(J):
                        for i in range(CM):
                            c, at = m * CM + i, slice(i * NB + j * P, i * NB + (j + 1) * P)
                            ins = products(banks[j][:, 0:S], ((hi[:, at], hT_hi[:, c, :]), (hi[:, at], hT_lo[:, c, :]),
                                                              (lo[:, at], hT_hi[:, c, :])), c == 0, c == C - 1)
                    ins.then_inc(used, 1)

            def rows(b, br, banks, left_hi, left_lo, before_chunk=None):
                for m in range(STAGES):
                    if before_chunk is not None:
                        before_chunk(m)
                    hi, lo = parts(b, br, m)
                    for i in range(CM):
                        c, at = m * CM + i, slice(i * NB, (i + 1) * NB)
                        for t, dst in enumerate(banks):
                            tt = slice(t * P, (t + 1) * P)
                            ins = products(dst[:, :], ((left_hi[:, c, tt], hi[:, at]), (left_hi[:, c, tt], lo[:, at]),
                                                       (left_lo[:, c, tt], hi[:, at])), c == 0, c == C - 1)
                    ins.then_inc(used, 1)

            def turned_chunks(m):
                pe.wait_ge(turned_dve, (m + 1) * CM // 2)

            for b in range(N_FIRST):
                if b in (2, 3, 4):
                    pe.wait_ge(proj_act, J * (b - 1))
                channels(b, b % 3, bank[4 * (b % 2):4 * (b % 2) + 4], turned_chunks if b == 0 else None)
            pe.wait_ge(proj_dve, J)
            with pe.Fori(0, N_HALVES) as f:
                b0, g, pa = f * 3 + N_FIRST, f * HALF_HEADS, f * 10 + 3 * J
                pe.wait_ge(att_copied, g + 2)
                channels(b0, N_FIRST % 3, bank[4:8])
                pe.wait_ge(att_copied, g + HALF_HEADS)
                pe.wait_ge(y_f32, J)
                channels(b0 + 1, (N_FIRST + 1) % 3, bank[0:4])

                def all_scores(m):
                    if m == 0:
                        pe.wait_ge(proj_act, pa + J)
                    if m != 1:
                        return
                    pe.wait_ge(proj_act, pa + 2 * J)
                    for h in range(HALF_HEADS):
                        dst = bank[SCORE_BANK[h]]
                        M.matmul(dst[:, 0:P], qT[:, h, 0:P], kT[:, h, 0:P], start=True, stop=True)
                        M.matmul(dst[:, P:SOFT], qT[:, h, P:S], kT[:, h, :], start=True, stop=True).then_inc(scores, 1)

                rows(b0 + 2, (N_FIRST + 2) % 3, bank[4:6], hT_hi, hT_lo, all_scores)
                for h in range(HALF_HEADS):
                    pe.wait_ge(probs_ready, g + (h + 1))
                    for i in range(3):
                        ins = M.transpose(bank[TURN_BANK[h]][:, i * P:(i + 1) * P], logits[:, h, i * P:(i + 1) * P], ident[:, :])
                    ins.then_inc(probs_turned, 1)
                pe.wait_ge(proj_act, pa + (2 * J + T))
                for h in range(HALF_HEADS):
                    pe.wait_ge(probsT_ready, g + (h + 1))
                    dst, hd = bank[OUT_BANK[h]], slice(h * P, (h + 1) * P)
                    M.matmul(dst[:, 0:P], v_tok[:, 0, hd], logits[:, h, 0:P], start=True, stop=True)
                    M.matmul(dst[:, P:S], v_tok[:, 0, hd], logits[:, h, P:2 * P], start=True, stop=False)
                    M.matmul(dst[:, P:S], v_tok[:, 1, hd], logits[:, h, 2 * P:SOFT], start=False, stop=True).then_inc(att_out, 1)

            pe.wait_ge(conv_done, 1)
            pe.wait_ge(att_copied, HALF_HEADS + N_HEADS)
            for j in range(J):
                ins = M.matmul(bank[4][:, 0:S], ones[:, :], cvT[:, j, :], start=(j == 0), stop=(j == J - 1))
            ins.then_inc(ln_mean, 1)

            pe.wait_ge(ya_ready, J)

            def layer_norm(m):
                if m == 1:
                    for j in range(J):
                        pe.wait_ge(ln_square, j + 1)
                        ins = M.matmul(bank[5][:, 0:S], ones[:, :], sqT[:, j, :], start=(j == 0), stop=(j == J - 1))
                    ins.then_inc(ln_var, 1)
                if m == 3:
                    pe.wait_ge(yc_ready, J)

            for i in range(D // NB):
                b = OUT_BLOCK0 + i
                if i == 2:
                    pe.wait_ge(ln_eps, 1)
                rows(b, b % 3, bank[2 * i:2 * i + 2], yT_hi, yT_lo, layer_norm if i == 0 else None)

            pe.wait_ge(mixed_added, 2 * (D // NB))
            pe.wait_ge(h_ready, 2 * T)
            turn_all(0, turned_h2)
            pe.wait_ge(turned_h2, C // 2)
            pe.wait_ge(turned_act, C // 2 + C // 2)
            pe.wait_ge(rw_ready, 2)
            W = GROUPS + E
            for c in range(C):
                ins = M.matmul(bank[5][0:W, 0:S], rw[:, c, :], h2T[:, c, :], start=(c == 0), stop=(c == C - 1))
            ins.then_inc(lt_done, 1)
            pe.wait_ge(lt_copied, 1)
            for t in range(T):
                ins = M.transpose(bank[4][:, t * W:(t + 1) * W], logitsT[:, t * P:(t + 1) * P], ident[0:W, 0:W])
            ins.then_inc(routed, 1)

            pe.wait_ge(chosen_ready, 1)
            pe.wait_ge(consts, CONSTS)
            for t in range(T):
                ins = M.matmul(bank[5][0:E, 0:P], chosen[:, 2, t, :], ones[:, :], start=(t == 0), stop=(t == T - 1))
            ins.then_inc(cnt_done, 1)
            pe.wait_ge(cnt_copied, 1)
            for t in range(T):
                dst = bank[4][:, 128 + t * E:128 + (t + 1) * E]
                M.matmul(dst, before[:, :], chosen[:, 2, t, :], start=True, stop=False)
                for tt in range(t):
                    M.matmul(dst, ones[:, :], chosen[:, 2, tt, :], start=False, stop=False)
                M.matmul(dst, cntT, before[0:E, 0:E], start=False, stop=True)
            M.matmul(bank[4][:, 192:192 + E], cntT, before[0:E, 0:E], start=True, stop=True)
            for t in range(T):
                ins = M.matmul(bank[4][:, 224:224 + E], ones[:, :], chosen[:, 2, t, :], start=(t == 0), stop=(t == T - 1))
            ins.then_inc(pos_done, 1)

            pe.wait_ge(pick_ready, T)
            pe.wait_ge(h2_lo_made, T)
            for c in range(C):
                if c >= 4:
                    pe.wait_ge(sorted_act if c % 2 else sorted_dve, (c - 4) // 2 + 1)
                for t in range(T):
                    M.matmul(bank[c % 4][:, :], h2_hi_c[:, t, c, :], pick[:, t, :], start=(t == 0), stop=False)
                    ins = M.matmul(bank[c % 4][:, :], h2_lo_c[:, t, c, :], pick[:, t, :], start=False, stop=(t == T - 1))
                ins.then_inc(sorted_done, 1)
            pe.wait_ge(sorted_act, C // 2)
            pe.wait_ge(sorted_dve, C // 2)

            def expert_in(which, b, br, before_chunk=None):
                rows(b, br, bank[which:which + 1], win_hi, win_lo, before_chunk)

            def turn_hidden(t):
                pe.wait_ge(hidden_ready, t + 1)
                for j in range(J):
                    ins = M.transpose(bank[2][:, j * P:(j + 1) * P],
                                      hidden[:, :].rearrange("p (k j) -> p j k", j=J)[:, j, :], ident[:, :])
                ins.then_inc(hidden_turned, 1)

            def down(t, b, br):
                pe.wait_ge(hiddenT_ready, t + 1)
                for j in range(J):
                    hi, lo = parts(b, br, j)
                    jj = slice(j * P, (j + 1) * P)
                    for n in range(D // NB):
                        if j == 0 and n == 0:
                            pe.wait_ge(y_act, ROWS_ACT * t + ROWS_ACT)
                        if j == 0 and n == ROWS_ACT:
                            pe.wait_ge(y_dve, ROWS_DVE * t + ROWS_DVE)
                        at = slice(n * NB, (n + 1) * NB)
                        ins = products(bank[4 + n][:, :], ((hiddenT_hi[:, jj], hi[:, at]), (hiddenT_hi[:, jj], lo[:, at]),
                                                           (hiddenT_lo[:, jj], hi[:, at])), j == 0, j == J - 1)
                    ins.then_inc(used, 1)

            expert_in(0, MOE_BLOCK0, MOE_BLOCK0 % 3, lambda m: pe.wait_ge(first_ready, m + 1))
            expert_in(1, MOE_BLOCK0 + 1, (MOE_BLOCK0 + 1) % 3)
            with pe.Fori(1, E) as e:
                b, br = g_block(e), (MOE_BLOCK0 + 2) % 3
                pe.wait_ge(win_ready, e)
                pe.wait_ge(silu_done, e)
                expert_in(0, b, br)
                turn_hidden(e - 1)
                expert_in(1, b + 1, br + 1)
                down(e - 1, b + 2, br + 2)
            turn_hidden(E - 1)
            down(E - 1, g_block(E), g_block(E) % 3)
            pe.wait_ge(tables_ready, 1)
            flag = pe.value_load(over_i[0:1, OVER:OVER + 1], min_val=0, max_val=E)
            with pe.If(flag > 0):
                with pe.Fori(E, E + OVER) as t:
                    b, br = over_block(t), OVER_BLOCK0 % 3
                    pe.wait_ge(win_ready, t)
                    expert_in(0, b, br)
                    expert_in(1, b + 1, br + 1)
                    turn_hidden(t)
                    down(t, b + 2, br + 2)


_INS = ["x", "norm1_g", "w_in", "conv_a_w", "conv_c_w", "conv_c_b", "ln_c_g", "ln_c_b", "w_out", "norm2_g",
        "router_g_w", "router_g_b", "router_e_w", "router_e_b", "w_gate", "w_up", "w_down", "final_g"]


def kernel(**inputs):
    import numpy as np
    import concourse.bacc as bacc
    from concourse.bass_utils import run_bass_kernel_spmd

    nc = bacc.Bacc("TRN2", target_bir_lowering=False, num_devices=1)
    arrays, aps = {}, {}
    for name in _INS:
        arr = np.ascontiguousarray(inputs[name])
        arrays[f"in_{name}"] = arr
        aps[name] = nc.dram_tensor(f"in_{name}", arr.shape, mybir.dt.from_np(arr.dtype), kind="ExternalInput").ap()
    out = nc.dram_tensor("out", (1, S, D), F32, kind="ExternalOutput").ap()
    y_sorted = nc.dram_tensor("y_sorted", (SLOTS, D), F32, kind="Internal").ap()
    hybrid_moe_program(nc, aps, out[0], y_sorted)
    result = run_bass_kernel_spmd(nc, [arrays], core_ids=[0])
    return result.results[0]["out"]
```
